# Optimizing a Trainium2 kernel written in Bass

```python
import math
import jax, jax.numpy as jnp
from jax import lax
import numpy as np

D_MODEL = 1024
BATCH = 1
SEQ = 512
DEPTH = 1

CHUNK = 64
N_META = 16
HEAD_DIM = 64
D_MIX = D_MODEL
A_HEADS = 8
A_KV_HEADS = 2
A_GROUP = A_HEADS // A_KV_HEADS
WINDOW = 128
WINDOW_CHUNKS = WINDOW // CHUNK
B_HEADS = 8
SB_BLOCK = 128
D_FF = 2816
EPS = 1e-6

A_Q = A_HEADS * HEAD_DIM
A_KV = A_KV_HEADS * HEAD_DIM
B_W = B_HEADS * HEAD_DIM
D_IN = A_Q + 2 * A_KV + 3 * B_W

kernel_name = "hymba_swa_sink_stickbreaking_macaron"

def rmsnorm(x, g):
    xf = x.astype(jnp.float32)
    y = xf * lax.rsqrt(jnp.mean(xf * xf, axis=-1, keepdims=True) + EPS)
    return (y * g.astype(jnp.float32)).astype(x.dtype)

def swiglu(x, w_gate, w_up, w_down):
    return (jax.nn.silu(x @ w_gate) * (x @ w_up)) @ w_down

def alibi_slopes(n_heads):
    return jnp.asarray(2.0 ** (-8.0 * np.arange(1, n_heads + 1) / n_heads), dtype=jnp.float32)

def swa_sink_attention(q, k, v, q_norm_g, k_norm_g, sinks):
    b, l = q.shape[0], q.shape[1]
    s = l - N_META
    nc = s // CHUNK
    scale = 1.0 / math.sqrt(HEAD_DIM)
    q = rmsnorm(q, q_norm_g)
    k = rmsnorm(k, k_norm_g)
    slopes = alibi_slopes(A_HEADS).reshape(A_KV_HEADS, A_GROUP)
    sink = sinks.astype(jnp.float32).reshape(A_KV_HEADS, A_GROUP)

    qm = q[:, :N_META].reshape(b, N_META, A_KV_HEADS, A_GROUP, HEAD_DIM)
    km, vm = k[:, :N_META], v[:, :N_META]
    qr = q[:, N_META:].reshape(b, nc, CHUNK, A_KV_HEADS, A_GROUP, HEAD_DIM)
    kr = k[:, N_META:].reshape(b, nc, CHUNK, A_KV_HEADS, HEAD_DIM)
    vr = v[:, N_META:].reshape(b, nc, CHUNK, A_KV_HEADS, HEAD_DIM)

    def band(t):
        tp = jnp.pad(t, ((0, 0), (WINDOW_CHUNKS - 1, 0), (0, 0), (0, 0), (0, 0)))
        return jnp.concatenate([tp[:, i:i + nc] for i in range(WINDOW_CHUNKS)], axis=2)
    kb, vb = band(kr), band(vr)
    wlen = WINDOW_CHUNKS * CHUNK

    qpos = (N_META + jnp.arange(s, dtype=jnp.int32)).reshape(nc, CHUNK)
    kpos_band = (N_META + (jnp.arange(nc, dtype=jnp.int32)[:, None] - (WINDOW_CHUNKS - 1)) * CHUNK
                 + jnp.arange(wlen, dtype=jnp.int32)[None, :])
    valid = kpos_band >= N_META
    dist_band = jnp.abs(qpos[:, :, None] - kpos_band[:, None, :]).astype(jnp.float32)
    dist_meta = (qpos[:, :, None] - jnp.arange(N_META, dtype=jnp.int32)[None, None, :]).astype(jnp.float32)

    sl = slopes[None, None, :, :, None, None]
    s_band = jnp.einsum('bcqhgd,bckhd->bchgqk', qr, kb).astype(jnp.float32) * scale
    s_band = s_band - sl * dist_band[None, :, None, None]
    s_band = jnp.where(valid[None, :, None, None, None, :], s_band, -jnp.inf)
    s_meta = jnp.einsum('bcqhgd,bmhd->bchgqm', qr, km).astype(jnp.float32) * scale
    s_meta = s_meta - sl * dist_meta[None, :, None, None]
    sink_r = jnp.broadcast_to(sink[None, None, :, :, None, None], s_meta.shape[:-1] + (1,))
    p = jax.nn.softmax(jnp.concatenate([s_meta, s_band, sink_r], axis=-1), axis=-1)
    p_meta = p[..., :N_META].astype(v.dtype)
    p_band = p[..., N_META:N_META + wlen].astype(v.dtype)
    o_r = (jnp.einsum('bchgqm,bmhd->bcqhgd', p_meta, vm)
           + jnp.einsum('bchgqk,bckhd->bcqhgd', p_band, vb)).reshape(b, s, A_Q)

    mpos = jnp.arange(N_META, dtype=jnp.int32)
    dist_mm = jnp.abs(mpos[:, None] - mpos[None, :]).astype(jnp.float32)
    s_mm = jnp.einsum('bqhgd,bkhd->bhgqk', qm, km).astype(jnp.float32) * scale
    s_mm = s_mm - slopes[None, :, :, None, None] * dist_mm
    sink_m = jnp.broadcast_to(sink[None, :, :, None, None], s_mm.shape[:-1] + (1,))
    p_mm = jax.nn.softmax(jnp.concatenate([s_mm, sink_m], axis=-1), axis=-1)[..., :N_META]
    o_m = jnp.einsum('bhgqk,bkhd->bqhgd', p_mm.astype(v.dtype), vm).reshape(b, N_META, A_Q)
    return jnp.concatenate([o_m, o_r], axis=1)

def stick_breaking_attention(q, k, v):
    b, l = q.shape[0], q.shape[1]
    nb = -(-l // SB_BLOCK)
    lp = nb * SB_BLOCK
    scale = 1.0 / math.sqrt(HEAD_DIM)
    qp = jnp.pad(q, ((0, 0), (0, lp - l), (0, 0), (0, 0)))
    q_blocks = qp.reshape(b, nb, SB_BLOCK, B_HEADS, HEAD_DIM).transpose(1, 0, 2, 3, 4)
    starts = jnp.arange(nb, dtype=jnp.int32) * SB_BLOCK
    kpos = jnp.arange(l, dtype=jnp.int32)
    kf = k.astype(jnp.float32)
    vf = v.astype(jnp.float32)

    def block(args):
        qb, q0 = args
        qpos = q0 + jnp.arange(SB_BLOCK, dtype=jnp.int32)
        z = jnp.einsum('bqhd,bkhd->bhqk', qb.astype(jnp.float32), kf) * scale
        mask = kpos[None, :] < qpos[:, None]
        log_keep = jnp.where(mask, jax.nn.log_sigmoid(-z), 0.0)
        after = lax.cumsum(log_keep, axis=3, reverse=True) - log_keep
        a = jnp.where(mask, jnp.exp(jax.nn.log_sigmoid(z) + after), 0.0)
        return jnp.einsum('bhqk,bkhd->bqhd', a, vf)

    o = lax.map(block, (q_blocks, starts))
    o = o.transpose(1, 0, 2, 3, 4).reshape(b, lp, B_W)[:, :l]
    return o.astype(q.dtype)

def hybrid_layer(h, ffn1_norm_g, ffn1_w_gate, ffn1_w_up, ffn1_w_down, mix_norm_g, w_in,
                 q_norm_g, k_norm_g, sinks, attn_out_g, sb_out_g, w_o,
                 ffn2_norm_g, ffn2_w_gate, ffn2_w_up, ffn2_w_down):
    b, l = h.shape[0], h.shape[1]
    h = h + 0.5 * swiglu(rmsnorm(h, ffn1_norm_g), ffn1_w_gate, ffn1_w_up, ffn1_w_down)
    proj = rmsnorm(h, mix_norm_g) @ w_in
    o1 = A_Q; o2 = o1 + A_KV; o3 = o2 + A_KV; o4 = o3 + B_W; o5 = o4 + B_W
    qa = proj[..., :o1].reshape(b, l, A_HEADS, HEAD_DIM)
    ka = proj[..., o1:o2].reshape(b, l, A_KV_HEADS, HEAD_DIM)
    va = proj[..., o2:o3].reshape(b, l, A_KV_HEADS, HEAD_DIM)
    qb = proj[..., o3:o4].reshape(b, l, B_HEADS, HEAD_DIM)
    kb = proj[..., o4:o5].reshape(b, l, B_HEADS, HEAD_DIM)
    vb = proj[..., o5:].reshape(b, l, B_HEADS, HEAD_DIM)
    out_a = swa_sink_attention(qa, ka, va, q_norm_g, k_norm_g, sinks)
    out_b = stick_breaking_attention(qb, kb, vb)
    mixed = jnp.concatenate([rmsnorm(out_a, attn_out_g), rmsnorm(out_b, sb_out_g)], axis=-1) @ w_o
    h = h + mixed
    h = h + 0.5 * swiglu(rmsnorm(h, ffn2_norm_g), ffn2_w_gate, ffn2_w_up, ffn2_w_down)
    return h

def setup_inputs(seed: int = 0) -> dict:
    key = jax.random.key(seed)
    ks = jax.random.split(key, 20)
    f32 = jnp.float32

    def w(k, shape, fan_in):
        return jax.random.normal(k, shape, f32) * (fan_in ** -0.5)

    def gain(k, shape):
        return 1.0 + 0.05 * jax.random.normal(k, shape, f32)

    return {
        "x": jax.random.normal(ks[0], (BATCH, SEQ, D_MODEL), f32),
        "meta_tokens": jax.random.normal(ks[1], (N_META, D_MODEL), f32),
        "ffn1_norm_g": gain(ks[2], (DEPTH, D_MODEL)),
        "ffn1_w_gate": w(ks[3], (DEPTH, D_MODEL, D_FF), D_MODEL),
        "ffn1_w_up": w(ks[4], (DEPTH, D_MODEL, D_FF), D_MODEL),
        "ffn1_w_down": w(ks[5], (DEPTH, D_FF, D_MODEL), D_FF),
        "mix_norm_g": gain(ks[6], (DEPTH, D_MODEL)),
        "w_in": w(ks[7], (DEPTH, D_MODEL, D_IN), D_MODEL),
        "q_norm_g": gain(ks[8], (DEPTH, HEAD_DIM)),
        "k_norm_g": gain(ks[9], (DEPTH, HEAD_DIM)),
        "sinks": 0.5 * jax.random.normal(ks[10], (DEPTH, A_HEADS), f32),
        "attn_out_g": gain(ks[11], (DEPTH, A_Q)),
        "sb_out_g": gain(ks[12], (DEPTH, B_W)),
        "w_o": w(ks[13], (DEPTH, D_MIX, D_MODEL), D_MIX),
        "ffn2_norm_g": gain(ks[14], (DEPTH, D_MODEL)),
        "ffn2_w_gate": w(ks[15], (DEPTH, D_MODEL, D_FF), D_MODEL),
        "ffn2_w_up": w(ks[16], (DEPTH, D_MODEL, D_FF), D_MODEL),
        "ffn2_w_down": w(ks[17], (DEPTH, D_FF, D_MODEL), D_FF),
    }

def reference(x, meta_tokens, ffn1_norm_g, ffn1_w_gate, ffn1_w_up, ffn1_w_down, mix_norm_g, w_in,
              q_norm_g, k_norm_g, sinks, attn_out_g, sb_out_g, w_o,
              ffn2_norm_g, ffn2_w_gate, ffn2_w_up, ffn2_w_down):
    b = x.shape[0]
    meta = jnp.broadcast_to(meta_tokens.astype(x.dtype)[None], (b, N_META, D_MODEL))
    h = jnp.concatenate([meta, x], axis=1)
    for i in range(DEPTH):
        h = hybrid_layer(h, ffn1_norm_g[i], ffn1_w_gate[i], ffn1_w_up[i], ffn1_w_down[i],
                         mix_norm_g[i], w_in[i], q_norm_g[i], k_norm_g[i], sinks[i],
                         attn_out_g[i], sb_out_g[i], w_o[i],
                         ffn2_norm_g[i], ffn2_w_gate[i], ffn2_w_up[i], ffn2_w_down[i])
    return h[:, N_META:]


_drawn_inputs = setup_inputs


def setup_inputs(seed=0):
    import zlib

    import numpy as np

    out = dict(_drawn_inputs(seed))
    spreads = {}
    factors = {'q_norm_g': 2.834, 'ffn2_norm_g': 3.951, 'sinks': 5.575}
    for name, (base, spread) in spreads.items():
        noise = np.random.default_rng([zlib.crc32(name.encode()), seed]).standard_normal(out[name].shape)
        drawn = base * np.exp(spread * noise) if base else spread * noise
        out[name] = __import__('jax').numpy.asarray(drawn.astype(out[name].dtype))
    for name, factor in factors.items():
        out[name] = (out[name] * factor).astype(out[name].dtype)
    return out
```

```python
from contextlib import ExitStack

import concourse.bass as bass
from concourse import mybir

ALU = mybir.AluOpType
ACT = mybir.ActivationFunctionType
AX = mybir.AxisListType
F32 = mybir.dt.float32
F32R = mybir.dt.float32r
BF16 = mybir.dt.bfloat16

P = 128
BANK = 512
HEAD_DIM = 64
CHUNK = 64
EPS = 1e-6
MASKED = 3e38
LN_EXP = "natural_log_exp_and_others"


def hybrid_layer_kernel(nc, x, meta_tokens, ffn1_norm_g, ffn1_w_gate, ffn1_w_up, ffn1_w_down, mix_norm_g, w_in,
                        q_norm_g, k_norm_g, sinks, attn_out_g, sb_out_g, w_o,
                        ffn2_norm_g, ffn2_w_gate, ffn2_w_up, ffn2_w_down, out):
    _, SEQ, D = x.shape
    N_META = meta_tokens.shape[0]
    T = SEQ + N_META
    HALF = T // 2
    F = ffn1_w_gate.shape[2]
    DC, FC = D // P, F // P
    TT = SEQ // P
    A_HEADS = sinks.shape[1]
    D_MIX = w_o.shape[1]
    B_HEADS = sb_out_g.shape[1] // HEAD_DIM
    A_Q = A_HEADS * HEAD_DIM
    D_IN = w_in.shape[2]
    B_W = B_HEADS * HEAD_DIM
    A_KV = (D_IN - A_Q - 3 * B_W) // 2
    A_KV_HEADS = A_KV // HEAD_DIM
    GROUP = A_HEADS // A_KV_HEADS
    QC, KC = A_Q // P, A_KV // P
    HC = B_W // P
    MC = D_MIX // P
    SCALE = HEAD_DIM ** -0.5
    assert (D, F, T, A_KV, GROUP, N_META) == (1024, 2816, 528, P, 4, 16) and FC % 2 == 0


    PAIR = 2 * DC * P
    FH = FC // 2
    DOWN = FH * P
    U_UP1 = 0
    U_DN1 = U_UP1 + FC
    U_IN = U_DN1 + 2 * DC
    U_WO = U_IN + D_IN // (2 * P)
    U_UP2 = U_WO + D // (2 * P)
    U_DN2 = U_UP2 + FC
    U_END = U_DN2 + 2 * DC

    def unit_size(n):
        return DOWN if U_DN1 <= n < U_IN or n >= U_DN2 else PAIR

    IN_CHUNKS = D_IN // P
    V_CHUNKS = KC + HC
    M_X = 0
    M_UP1 = M_X + DC
    M_DN1 = M_UP1 + 2 * FC + 2
    M_IN = M_DN1 + 2 * DC
    C_KA, C_VA, C_QB, C_KB, C_VB = QC, QC + KC, QC + 2 * KC, QC + 2 * KC + HC, QC + 2 * KC + 2 * HC
    in_uses = [("chunk", 0), ("norm", 0), ("norm", 1)]
    for c in range(1, IN_CHUNKS):
        in_uses.append(("chunk", c))
        if C_KB - 1 <= c < C_KB + QC + KC - 1:
            in_uses.append(("qk", c - C_KB + 1))
        if c == C_VB:
            in_uses.append(("v", 0))
        elif c > C_VB:
            in_uses.append(("v", c - C_VB))
    in_uses.append(("v", HC))
    m_in = {use: M_IN + k for k, use in enumerate(in_uses)}
    M_OUT_NORM = M_IN + len(in_uses)
    M_WO = M_OUT_NORM + 2
    M_UP2 = M_WO + DC
    M_DN2 = M_UP2 + 2 * FC + 2

    EDGE = CHUNK + N_META
    A_KEYS = P + EDGE
    B_COLS = [2 * P + P, 3 * P, 4 * P, SEQ]
    B_ROWS = [P, P, P, N_META]
    B_PARTS = [[(2, 0), (3, 2 * P)], [(1, 0)], [(0, 0)]]
    UNITS = TT * A_KV_HEADS
    assert UNITS == B_HEADS and TT == 4

    with ExitStack() as ctx:
        def sb(name, shape, dt=F32, side="left", into=None):
            return (into or ctx).enter_context(nc.sbuf_tensor(name, shape, dt, side=side))

        def sem(name):
            return ctx.enter_context(nc.semaphore(name))

        raw = [sb(f"raw{s}", [P, PAIR]) for s in range(2)]
        w_hi = [sb(f"w_hi{s}", [P, PAIR], F32R) for s in range(2)]
        w_lo = [sb(f"w_lo{s}", [P, PAIR], F32R) for s in range(2)]
        h = sb("h", [P, DC, T])
        rms_inv = sb("rms_inv", [P, T])
        sq_sum = sb("sq_sum", [P, T])
        tmp_a = [sb(f"tmp_a{s}", [P, T]) for s in range(2)]
        tmp_b = [sb(f"tmp_b{s}", [P, T]) for s in range(2)]
        ident = sb("ident", [P, P])
        ones = sb("ones", [P, P])
        G_FFN1, G_MIX, G_FFN2, G_OUT = 0, DC, 2 * DC, 3 * DC
        GAINS = 3 * DC + MC + 2
        gain_rows = sb("gain_rows", [GAINS, P])
        gains = sb("gains", [P, GAINS])
        head_gain = gains[:, GAINS - 2:GAINS]
        sink_col = sb("sink_col", [P, A_HEADS])

        right, left = ExitStack(), ExitStack()
        x_hi = sb("x_hi", [P, DC, T], F32R, "right", right)
        x_lo = sb("x_lo", [P, DC, T], F32R, "right", right)
        x_in = sb("x_in", [P, TT, D], into=left)
        meta_in = sb("meta_in", [N_META, D], into=left)
        left.close()
        left = ExitStack()
        g1_hi = sb("g1_hi", [P, FC, T], F32R, into=left)
        g1_lo = sb("g1_lo", [P, FC, T], F32R, into=left)
        left.close()
        left, v_only = ExitStack(), ExitStack()
        qa = sb("qa", [P, QC, T], into=left)
        k_a = sb("k_a", [P, T], into=left)
        k_dup = [sb(f"k_dup{g}", [P, T], into=left) for g in range(A_KV_HEADS)]
        qb = sb("qb", [P, HC, T], into=left)
        kb = sb("kb", [P, HC, T], into=left)
        v_nat = sb("v_nat", [P, V_CHUNKS, TT, P], into=left)
        v_meta = sb("v_meta", [N_META, V_CHUNKS, P], into=left)
        v_edge = sb("v_edge", [EDGE, TT, P], into=left)
        mix_hi = sb("mix_hi", [P, MC, SEQ], F32R, into=left)
        mix_lo = sb("mix_lo", [P, MC, SEQ], F32R, into=left)
        row_max = sb("row_max", [P, GROUP], into=left)
        neg_max = sb("neg_max", [P, GROUP], into=left)
        sink_exp = sb("sink_exp", [P, GROUP], into=left)
        row_sum = sb("row_sum", [P, GROUP], into=left)
        head_ones = sb("head_ones", [P, P], into=left)
        neg_ones = sb("neg_ones", [P, P], into=left)
        neg_tri = sb("neg_tri", [P, P], into=left)
        causal = sb("causal", [P, P], into=left)
        ident_bf = sb("ident_bf", [P, P], BF16, into=left)
        future_bf = sb("future_bf", [P, P], BF16, into=left)
        dist = sb("dist", [P, TT, A_KEYS], into=left)
        v_t = sb("v_t", [P, V_CHUNKS, T], into=v_only)
        v_only.close()
        right.close()
        right = ExitStack()
        mixed = sb("mixed", [P, MC, SEQ], side="right", into=right)
        sp = [sb(f"sp{j}", [B_ROWS[j], B_COLS[j]], side="right", into=right) for j in range(4)]
        stick = [sb(f"stick{j}", [B_ROWS[j], B_COLS[j]], side="right", into=right) for j in range(4)]
        carry = [None] + [sb(f"carry{j}", [P, j * P + P], side="right", into=right) for j in range(1, 4)]
        probs = sb("probs", [P, GROUP, A_KEYS], side="right", into=right)
        p_own = sb("p_own", [P, GROUP, P], side="right", into=right)
        p_edge = sb("p_edge", [EDGE, GROUP, P], side="right", into=right)
        right.close()
        left.close()
        left, right = ExitStack(), ExitStack()
        g2_hi = sb("g2_hi", [P, FC, SEQ], F32R, into=left)
        g2_lo = sb("g2_lo", [P, FC, SEQ], F32R, into=left)
        x2_hi = sb("x2_hi", [P, DC, SEQ], F32R, "right", right)
        x2_lo = sb("x2_lo", [P, DC, SEQ], F32R, "right", right)
        left.close()
        right.close()

        ps = ctx.enter_context(nc.psum_tensor("ps", [P, 8, BANK], F32))
        z_bank = [ps[0:B_ROWS[j], j, 0:B_COLS[j]] for j in range(4)]

        def slot(m, cols):
            b = 2 * (m % 4)
            return ps[:, b, 0:SEQ] if cols == SEQ else ps[:, b:b + 2, 0:HALF]

        def wide(ap, cols):
            return ap if cols == SEQ else ap.rearrange("p (a b) -> p a b", b=HALF)

        def tok(t, c, cols):
            row = t[:, bass.ds(c, 1), 0:cols].rearrange("p a b -> p (a b)")
            return wide(row, cols)

        raw_loaded = [sem(f"raw_loaded{s}") for s in range(2)]
        hi_split, lo_split = sem("hi_split"), sem("lo_split")
        acc_full, evacuated = sem("acc_full"), sem("evacuated")
        x_loaded, meta_loaded, small_loaded = sem("x_loaded"), sem("meta_loaded"), sem("small_loaded")
        const_step, const_done = sem("const_step"), sem("const_done")
        x_hi_done, x_lo_done = sem("x_hi_done"), sem("x_lo_done")
        sq_done, sq_added = sem("sq_done"), sem("sq_added")
        mean_done, inv_done, rms_done = sem("mean_done"), sem("inv_done"), sem("rms_done")
        silu_done, hidden_done, g_hi_done, g_lo_done = (
            sem(k) for k in ("silu_done", "hidden_done", "g_hi_done", "g_lo_done"))
        v_edge_done = sem("v_edge_done")
        qk_squared, qk_mean, qk_inv, qk_rms, qk_scaled, qk_done = (
            sem(k) for k in ("qk_squared", "qk_mean", "qk_inv", "qk_rms", "qk_scaled", "qk_done"))
        a_scores, a_biased, a_max, a_sink_max, a_neg = (sem(k) for k in ("a_scores", "a_biased", "a_max",
                                                                        "a_sink_max", "a_neg"))
        a_sink_in, a_exp, a_total, a_inv, a_probs = (sem(k) for k in ("a_sink_in", "a_exp", "a_total", "a_inv",
                                                                     "a_probs"))
        a_turned, a_pt, a_out, a_mixed = (sem(k) for k in ("a_turned", "a_pt", "a_out", "a_mixed"))
        b_scores, b_abs, b_exp, b_ln, b_soft = (sem(k) for k in ("b_scores", "b_abs", "b_exp", "b_ln", "b_soft"))
        b_masked, b_summed, b_carry, b_logs, b_stick, b_out, b_mixed = (
            sem(k) for k in ("b_masked", "b_summed", "b_carry", "b_logs", "b_stick", "b_out", "b_mixed"))
        on_sq, on_added, on_sum, on_mean, on_inv, on_rms, on_scaled, on_hi, on_lo = (
            sem(k) for k in ("on_sq", "on_added", "on_sum", "on_mean", "on_inv", "on_rms", "on_scaled", "on_hi",
                             "on_lo"))
        out_turned, out_staged = sem("out_turned"), sem("out_staged")
        gains_turned, gains_done, dist_done = sem("gains_turned"), sem("gains_done"), sem("dist_done")
        SMALL = 16 * 10
        out_written = [sem(f"out_written{s}") for s in range(2)]

        def full_after(n):
            for base, m in ((U_DN2, M_DN2), (U_UP2, M_UP2), (U_WO, M_WO), (U_IN, M_IN), (U_DN1, M_DN1),
                            (U_UP1, M_UP1)):
                if n >= base:
                    k = n - base
                    if base == U_IN:
                        return m_in["chunk", 2 * k + 1] + 1
                    return m + {U_DN1: k + 1, U_DN2: k + 1, U_WO: 2 * k + 2}.get(base, 2 * k + 4)

        def pair_src(n0, dy):
            r = raw[n0 % 2]
            pair = r.rearrange("p (c w o) -> p c w o", c=DC, w=2)
            for base, w_gate, w_up in ((U_UP1, ffn1_w_gate, ffn1_w_up), (U_UP2, ffn2_w_gate, ffn2_w_up)):
                if base <= n0 < base + FC:
                    cols = bass.ds((n0 - base + 2 * dy) * P, P)
                    return [(pair[:, :, w, :], src[0].rearrange("(c p) n -> p c n", p=P)[:, :, cols])
                            for w, src in enumerate((w_gate, w_up))]
            src, base = (w_in, U_IN) if n0 < U_WO else (w_o, U_WO)
            cols = bass.ds((n0 - base + 2 * dy) * 2 * P, 2 * P)
            view = src[0].rearrange("(c p) n -> p c n", p=P)[:, :, cols]
            whole = r.rearrange("p (c n) -> p c n", c=DC)
            return [(whole[:, q * DC // 2:(q + 1) * DC // 2, :], view[:, q * DC // 2:(q + 1) * DC // 2, :])
                    for q in range(2)]

        def down_src(n0, dy):
            base, src = (U_DN1, ffn1_w_down) if n0 < U_IN else (U_DN2, ffn2_w_down)
            half = (n0 - base) % 2
            cols = bass.ds(((n0 - base) // 2 + dy) * P, P)
            view = src[0].rearrange("(c p) n -> p c n", p=P)[:, half * FH:(half + 1) * FH, cols]
            r = raw[n0 % 2][:, 0:DOWN].rearrange("p (c n) -> p c n", c=FH)
            return [(r[:, a:b, :], view[:, a:b, :]) for a, b in ((0, 6), (6, FH))]

        def placed(n0, dy):
            return (n0 + 2 * dy, 0) if isinstance(dy, int) else (n0, dy)

        def load(sync, n0, dy=0):
            if n0 >= 2 or not isinstance(dy, int):
                sync.wait_ge(lo_split, n0 - 1 + 2 * dy)
            for dst, src in (pair_src(n0, dy) if unit_size(n0) == PAIR else down_src(n0, dy)):
                sync.dma_start(dst, src).then_inc(raw_loaded[n0 % 2], 16)

        def split_hi(act, n0, dy=0, step=4):
            n0, dy = placed(n0, dy)
            if n0 >= U_END:
                return
            s, size = n0 % 2, unit_size(n0)
            act.wait_ge(raw_loaded[s], 32 * (n0 // 2 + 1) + 32 * dy)
            if not isinstance(dy, int):
                act.wait_ge(acc_full, full_after(n0) - step + step * dy)
            elif n0 >= 2:
                act.wait_ge(acc_full, full_after(n0 - 2))
            act.activation(w_hi[s][:, 0:size], raw[s][:, 0:size], ACT.Copy).then_inc(hi_split, 1)

        def split_lo(dve, n0, dy=0):
            n0, dy = placed(n0, dy)
            if n0 >= U_END:
                return
            s, size = n0 % 2, unit_size(n0)
            dve.wait_ge(hi_split, n0 + 1 + 2 * dy)
            dve.tensor_tensor(w_lo[s][:, 0:size], raw[s][:, 0:size], w_hi[s][:, 0:size].bitcast(F32),
                              ALU.subtract).then_inc(lo_split, 1)

        def passes(pe, m, cols, left_hi, left_lo, right_hi, right_lo, start, stop):
            dst = slot(m, cols)
            parts = [(dst, slice(0, SEQ))] if cols == SEQ else [
                (dst[:, a, :], slice(a * HALF, (a + 1) * HALF)) for a in range(2)]
            trio = ((left_hi, right_hi), (left_hi, right_lo), (left_lo, right_hi))
            for k, (lt, rt) in enumerate(trio):
                for o, r in parts:
                    last = pe.matmul(o, lt, rt[:, r], start=start and k == 0, stop=stop and k == 2)
            return last

        def pair_chunk(pe, m, n0, which, cols, rh, rl, dm=0, dy=0, fresh=None):
            s = n0 % 2
            if which == 0:
                pe.wait_ge(lo_split, n0 + 1 + 2 * dy)
            pe.wait_ge(evacuated, m - 3 + 4 * dm)
            whi = w_hi[s].rearrange("p (c w o) -> p c w o", c=DC, w=2)
            wlo = w_lo[s].rearrange("p (c w o) -> p c w o", c=DC, w=2)
            for c in range(DC):
                if fresh is not None:
                    pe.wait_ge(fresh[0], fresh[1] + c + 1)
                last = passes(pe, m, cols, whi[:, c, which, :], wlo[:, c, which, :], rh[:, c, :], rl[:, c, :],
                              c == 0, c == DC - 1)
            last.then_inc(acc_full, 1)

        def norm_sum(pe, m, cols, sums):
            pe.wait_ge(sq_added, sums)
            pe.wait_ge(evacuated, m - 2)
            dst = slot(m, cols)
            if cols == SEQ:
                last = pe.matmul(dst, ones[:, :], sq_sum[:, 0:SEQ], start=True, stop=True)
            else:
                for a in range(2):
                    last = pe.matmul(dst[:, a, :], ones[:, :], sq_sum[:, a * HALF:(a + 1) * HALF],
                                     start=True, stop=True)
            last.then_inc(acc_full, 2)

        def pe_first_unit(pe, n0, m0, cols, rh, rl, done):
            pair_chunk(pe, m0, n0, 0, cols, rh, rl, fresh=(x_lo_done, done))
            norm_sum(pe, m0 + 1, cols, done + DC)
            pair_chunk(pe, m0 + 3, n0, 1, cols, rh, rl)

        def pe_up(pe, n0, m0, cols, rh, rl, done):
            pe_first_unit(pe, n0, m0, cols, rh, rl, done)
            for w in range(2):
                pair_chunk(pe, m0 + 4 + w, n0 + 1, w, cols, rh, rl)
            with pe.Fori(1, FH) as it:
                for k in range(2):
                    for w in range(2):
                        pair_chunk(pe, m0 + 2 + 2 * k + w, n0 + k, w, cols, rh, rl, dm=it, dy=it)

        def pe_down_chunk(pe, m, n0, cols, gh, gl, dm=0):
            for half in range(2):
                s = (n0 + half) % 2
                pe.wait_ge(lo_split, n0 + half + 1 + 4 * dm)
                if half == 0:
                    pe.wait_ge(evacuated, m - 3 + 4 * dm)
                for c in range(FH):
                    f = half * FH + c
                    last = passes(pe, m, cols, w_hi[s][:, c * P:(c + 1) * P], w_lo[s][:, c * P:(c + 1) * P],
                                  gh[:, f, :], gl[:, f, :], f == 0, f == FC - 1)
                last.then_inc(acc_full, 1)

        def finish_hi(act, g0, n, par, c, cols, xh, ready):
            if not isinstance(n, int) or n >= 2:
                act.wait_ge(sq_added, n - 1)
            act.wait_ge(evacuated, ready)
            act.activation(tok(xh, c, cols), tok(h, c, cols), ACT.Copy,
                           scale=gains[:, bass.ds(c + g0, 1)]).then_inc(x_hi_done, 1)
            act.activation(wide(tmp_a[par][:, 0:cols], cols), tok(h, c, cols), ACT.Square).then_inc(sq_done, 1)

        def finish_lo(dve, g0, n, c, cols, xh, xl):
            dve.wait_ge(x_hi_done, n + 1)
            dve.scalar_tensor_tensor(tok(xl, c, cols), tok(h, c, cols), gains[:, bass.ds(c + g0, 1)],
                                     tok(xh, c, cols).bitcast(F32), ALU.mult, ALU.subtract).then_inc(x_lo_done, 1)

        def finish_sum(pool, n, par, cols, first=False, taken=None):
            pool.wait_ge(sq_done, n + 1)
            if first:
                if taken:
                    pool.wait_ge(*taken)
                pool.tensor_copy(sq_sum[:, 0:cols], tmp_a[par][:, 0:cols]).then_inc(sq_added, 1)
            else:
                pool.wait_ge(sq_added, n)
                pool.tensor_tensor(sq_sum[:, 0:cols], sq_sum[:, 0:cols], tmp_a[par][:, 0:cols],
                                   ALU.add).then_inc(sq_added, 1)

        def rms_dve(dve, m, cols, k):
            dve.wait_ge(acc_full, m + 1)
            dve.tensor_scalar(wide(rms_inv[:, 0:cols], cols), slot(m, cols), 1.0 / D, EPS,
                              ALU.mult, ALU.add).then_inc(mean_done, 1)
            dve.wait_ge(mean_done, k + 1)
            dve.reciprocal(rms_inv[:, 0:cols], rms_inv[:, 0:cols]).then_inc(inv_done, 1)

        def rms_act(act, cols, k):
            act.wait_ge(inv_done, k + 1)
            act.activation(rms_inv[:, 0:cols], rms_inv[:, 0:cols], ACT.Sqrt).then_inc(rms_done, 1)

        def scale_gate(dve, m, par, cols, dm=0, frees=1):
            dve.wait_ge(acc_full, m + 1 + 4 * dm)
            dve.tensor_tensor(wide(tmp_a[par][:, 0:cols], cols), slot(m, cols), wide(rms_inv[:, 0:cols], cols),
                              ALU.mult).then_inc(evacuated, frees)

        def scale_up(dve, m, par, cols, dm=0):
            dve.wait_ge(acc_full, m + 1 + 4 * dm)
            dve.tensor_tensor(wide(tmp_b[par][:, 0:cols], cols), slot(m, cols), wide(rms_inv[:, 0:cols], cols),
                              ALU.mult).then_inc(evacuated, 1)

        def hidden(dve, f0, m, k0, cols, dm=0, dk=0):
            par = k0 % 2
            dve.wait_ge(silu_done, f0 + k0 + 1 + 2 * dk)
            dve.wait_ge(evacuated, m + 1 + 4 * dm)
            dve.tensor_tensor(tmp_b[par][:, 0:cols], tmp_a[par][:, 0:cols], tmp_b[par][:, 0:cols],
                              ALU.mult).then_inc(hidden_done, 1)

        def hidden_lo(dve, f0, k0, cols, gh, gl, dk=0):
            dve.wait_ge(g_hi_done, f0 + k0 + 1 + 2 * dk)
            dve.tensor_tensor(gl[:, bass.ds(k0 + 2 * dk, 1), 0:cols].rearrange("p a b -> p (a b)"),
                              tmp_b[k0 % 2][:, 0:cols],
                              gh[:, bass.ds(k0 + 2 * dk, 1), 0:cols].rearrange("p a b -> p (a b)").bitcast(F32),
                              ALU.subtract).then_inc(g_lo_done, 1)

        def act_hidden(act, f0, m, k0, cols, gh, dm=0, dk=0):
            par = k0 % 2
            act.wait_ge(evacuated, m + 1 + 4 * dm)
            act.activation(tmp_a[par][:, 0:cols], tmp_a[par][:, 0:cols], ACT.Silu).then_inc(silu_done, 1)
            act.wait_ge(hidden_done, f0 + k0 + 1 + 2 * dk)
            act.activation(gh[:, bass.ds(k0 + 2 * dk, 1), 0:cols].rearrange("p a b -> p (a b)"),
                           tmp_b[par][:, 0:cols], ACT.Copy).then_inc(g_hi_done, 1)

        def act_up(act, n0, m0, f0, cols, gh, norm):
            def unit(k, dy=0):
                split_hi(act, n0 + k + 1, dy)
                act_hidden(act, f0, m0 + 2 + 2 * k, k, cols, gh, dm=dy, dk=dy)

            split_hi(act, n0 + 1)
            rms_act(act, cols, norm)
            act.preload_act_table_set("silu_and_others")
            act_hidden(act, f0, m0, 0, cols, gh)
            unit(1)
            with act.Fori(1, FH - 1) as it:
                unit(0, it)
                unit(1, it)
            unit(FC - 2)
            unit(FC - 1)

        def dve_up(dve, n0, m0, f0, cols, gh, gl, norm):
            def unit(k, dy=0):
                m = m0 + 2 + 2 * k
                split_lo(dve, n0 + k + 1, dy)
                scale_gate(dve, m, k % 2, cols, dm=dy)
                if k:
                    hidden_lo(dve, f0, k - 1, cols, gh, gl, dk=dy)
                else:
                    hidden_lo(dve, f0, 1, cols, gh, gl, dk=dy - 1)
                scale_up(dve, m + 1, k % 2, cols, dm=dy)
                hidden(dve, f0, m + 1, k, cols, dm=dy, dk=dy)

            split_lo(dve, n0 + 1)
            rms_dve(dve, m0 + 1, cols, norm)
            dve.wait_ge(rms_done, norm + 1)
            scale_gate(dve, m0, 0, cols, frees=3)
            scale_up(dve, m0 + 3, 0, cols)
            hidden(dve, f0, m0 + 3, 0, cols)
            unit(1)
            with dve.Fori(1, FH - 1) as it:
                unit(0, it)
                unit(1, it)
            unit(FC - 2)
            unit(FC - 1)
            hidden_lo(dve, f0, FC - 1, cols, gh, gl)

        def a_heads(u):
            for r in range(GROUP):
                hd = GROUP * (u % A_KV_HEADS) + r
                yield r, hd, hd // 2, HEAD_DIM * (hd % 2)

        def pe_a_scores(pe, u):
            t = u // A_KV_HEADS
            if u:
                pe.wait_ge(a_pt, 2 * u)
            keys = k_dup[u % A_KV_HEADS]
            prev = max(t * P - CHUNK, 0)
            for r, hd, c, o in a_heads(u):
                lt = qa[o:o + HEAD_DIM, c, t * P:(t + 1) * P]
                at = A_KEYS * (r // 2)
                for lo, src, w in ((0, t * P, P), (P, prev, CHUNK), (P + CHUNK, SEQ, N_META)):
                    last = pe.matmul(ps[:, 5 + r % 2, at + lo:at + lo + w], lt, keys[o:o + HEAD_DIM, src:src + w],
                                     start=True, stop=True)
            last.then_inc(a_scores, 1)

        def pe_a_turn(pe, u):
            pe.wait_ge(a_probs, u + 1)
            for r in range(GROUP):
                pe.transpose(ps[:, 5, r * P:(r + 1) * P], probs[:, r, 0:P], ident[:, :])
                last = pe.transpose(ps[0:EDGE, 6, r * P:(r + 1) * P], probs[:, r, P:A_KEYS], ident[:, :])
            last.then_inc(a_turned, 1)

        def pe_a_out(pe, u):
            t, o = u // A_KV_HEADS, HEAD_DIM * (u % A_KV_HEADS)
            pe.wait_ge(a_pt, 2 * u + 2)
            if u:
                pe.wait_ge(a_mixed, u)
            dst = ps[0:HEAD_DIM, 7, 0:GROUP * P]
            pe.matmul(dst, v_nat[:, 0, t, o:o + HEAD_DIM], p_own.rearrange("p r q -> p (r q)"),
                      start=True, stop=False)
            pe.matmul(dst, v_edge[:, t, o:o + HEAD_DIM], p_edge.rearrange("p r q -> p (r q)"),
                      start=False, stop=True).then_inc(a_out, 1)

        def dve_a_max(dve, u):
            t = u // A_KV_HEADS
            dve.wait_ge(a_scores, u + 1)
            for r, hd, c, o in a_heads(u):
                at = A_KEYS * (r // 2)
                dve.scalar_tensor_tensor(probs[:, r, :], dist[:, t, :], -(2.0 ** (-8.0 * (hd + 1) / A_HEADS)),
                                         ps[:, 5 + r % 2, at:at + A_KEYS], ALU.mult, ALU.add).then_inc(a_biased, 1)
            dve.wait_ge(a_biased, GROUP * (u + 1))
            sinks_u = sink_col[:, GROUP * (u % A_KV_HEADS):GROUP * (u % A_KV_HEADS + 1)]
            dve.tensor_reduce(row_max[:, :], probs[:, :, :], AX.X, ALU.max).then_inc(a_max, 1)
            dve.wait_ge(a_max, u + 1)
            dve.tensor_tensor(row_max[:, :], row_max[:, :], sinks_u, ALU.max).then_inc(a_sink_max, 1)
            dve.wait_ge(a_sink_max, u + 1)
            dve.tensor_scalar(neg_max[:, :], row_max[:, :], -1.0, None, ALU.mult).then_inc(a_neg, 1)
            dve.wait_ge(a_neg, u + 1)
            dve.tensor_tensor(sink_exp[:, :], neg_max[:, :], sinks_u, ALU.add).then_inc(a_sink_in, 1)

        def act_a_exp(act, u):
            act.wait_ge(a_sink_in, u + 1)
            for r in range(GROUP):
                act.activation(probs[:, r, :], probs[:, r, :], ACT.Exp, bias=neg_max[:, r:r + 1],
                               accum_out=row_sum[:, r:r + 1])
            act.activation(sink_exp[:, :], sink_exp[:, :], ACT.Exp).then_inc(a_exp, 1)

        def dve_a_probs(dve, u):
            dve.wait_ge(a_exp, u + 1)
            dve.tensor_tensor(row_sum[:, :], row_sum[:, :], sink_exp[:, :], ALU.add).then_inc(a_total, 1)
            dve.wait_ge(a_total, u + 1)
            dve.reciprocal(row_sum[:, :], row_sum[:, :]).then_inc(a_inv, 1)
            dve.wait_ge(a_inv, u + 1)
            dve.tensor_tensor(probs[:, :, :], probs[:, :, :],
                              row_sum[:, :].unsqueeze(2).to_broadcast([P, GROUP, A_KEYS]), ALU.mult).then_inc(a_probs, 1)

        def act_a_pt(act, u):
            act.wait_ge(a_turned, u + 1)
            if u:
                act.wait_ge(a_out, u)
            act.activation(p_own.rearrange("p r q -> p (r q)"), ps[:, 5, :], ACT.Copy).then_inc(a_pt, 1)
            act.activation(p_edge.rearrange("p r q -> p (r q)"), ps[0:EDGE, 6, :], ACT.Copy).then_inc(a_pt, 1)

        def dve_a_mixed(dve, u):
            t, g = u // A_KV_HEADS, u % A_KV_HEADS
            dve.wait_ge(a_out, u + 1)
            src = ps[0:HEAD_DIM, 7, :].rearrange("d (c e q) -> d c e q", c=GROUP // 2, e=2)
            for e in range(2):
                c0 = g * GROUP // 2
                last = dve.tensor_copy(mixed[e * HEAD_DIM:(e + 1) * HEAD_DIM, c0:c0 + GROUP // 2, t * P:(t + 1) * P],
                                       src[:, :, e, :])
            last.then_inc(a_mixed, 1)

        def pe_b_scores(pe, hd):
            c, o = hd // 2, HEAD_DIM * (hd % 2)
            q = qb[o:o + HEAD_DIM, c, :]
            k = kb[o:o + HEAD_DIM, c, :]
            for j in range(4):
                if hd:
                    pe.wait_ge(b_stick, 4 * (hd - 1) + j + 1)
                if j == 3:
                    last = pe.matmul(z_bank[3], k[:, SEQ:T], q[:, 0:SEQ], start=True, stop=False,
                                     skip_group_check=True)
                else:
                    for n, (kt, at) in enumerate(B_PARTS[j]):
                        w = SEQ - kt * P
                        last = pe.matmul(z_bank[j][:, at:at + w], k[:, kt * P:(kt + 1) * P], q[:, kt * P:SEQ],
                                         start=n == 0, stop=False, skip_group_check=True)
                last.then_inc(b_scores, 1)

        def pe_b_logs(pe, hd):
            for j in range(4):
                if j == 3:
                    pe.wait_ge(b_soft, 4 * hd + 4)
                else:
                    pe.wait_ge(b_masked, 3 * hd + j + 1)
                if j:
                    pe.wait_ge(b_carry, 3 * hd + j)
                rows = B_ROWS[j]
                acc = dict(start=False, skip_group_check=True)
                if j == 0:
                    pe.matmul(z_bank[0][:, P:2 * P], neg_ones[:, :], sp[0][:, 2 * P:3 * P], stop=False, **acc)
                else:
                    w = P * (j + 1) if j < 3 else SEQ
                    first = B_COLS[j] - w
                    pe.matmul(z_bank[j][:, first:first + w], neg_ones[:, 0:rows], carry[j][:, 0:w], stop=False, **acc)
                if j < 3:
                    for kt, at in B_PARTS[j]:
                        pe.matmul(z_bank[j][:, at:at + P], ident_bf[:, :], future_bf[:, :], stop=False, **acc)
                last = pe.matmul(z_bank[j], neg_tri[0:rows, 0:rows], sp[j][:, :], stop=True, **acc)
                last.then_inc(b_logs, 1)

        def pe_b_out(pe, hd):
            c, o = 1 + hd // 2, HEAD_DIM * (hd % 2)
            pe.wait_ge(b_stick, 4 * hd + 4)
            if hd:
                pe.wait_ge(b_mixed, hd)
            acc = dict(skip_group_check=True)
            for j in (2, 1, 0):
                for kt, at in B_PARTS[j]:
                    w = SEQ - kt * P
                    pe.matmul(ps[0:HEAD_DIM, 4, kt * P:SEQ], v_nat[:, c, kt, o:o + HEAD_DIM],
                              stick[j][:, at:at + w], start=j == 2, stop=False, **acc)
            pe.matmul(ps[0:HEAD_DIM, 4, :], v_meta[:, c, o:o + HEAD_DIM], stick[3][:, :],
                      start=False, stop=True, **acc).then_inc(b_out, 1)

        def act_b_ln(act, hd):
            for j in range(4):
                act.wait_ge(b_scores, 4 * hd + j + 1)
                if hd and j == 0:
                    act.wait_ge(b_logs, 4 * hd)
                    act.wait_ge(b_carry, 3 * hd)
                act.activation(sp[j][:, :], z_bank[j], ACT.Abs).then_inc(b_abs, 1)
                act.wait_ge(b_abs, 4 * hd + j + 1)
                act.activation(sp[j][:, :], sp[j][:, :], ACT.Exp, scale=-1.0).then_inc(b_exp, 1)
                act.wait_ge(b_exp, 4 * hd + j + 1)
                act.activation(sp[j][:, :], sp[j][:, :], ACT.Ln, bias=1.0).then_inc(b_ln, 1)

        def dve_b_soft(dve, hd):
            for j in range(4):
                dve.wait_ge(b_ln, 4 * hd + j + 1)
                dve.scalar_tensor_tensor(sp[j][:, :], z_bank[j], 0.0, sp[j][:, :], ALU.max,
                                         ALU.add).then_inc(b_soft, 1)

        def pool_b(pool, hd):
            for j in range(3):
                pool.wait_ge(b_soft, 4 * hd + j + 1)
                for kt, at in B_PARTS[j]:
                    last = pool.tensor_tensor(sp[j][:, at:at + P], sp[j][:, at:at + P], causal[:, :], ALU.mult)
                last.then_inc(b_masked, 1)
                pool.wait_ge(b_masked, 3 * hd + j + 1)
                if hd:
                    pool.wait_ge(b_logs, 4 * hd)
                nxt = carry[j + 1]
                w = B_COLS[j] if j else 2 * P
                if j == 0:
                    pool.tensor_copy(nxt[:, 0:P], sp[0][:, 0:P])
                    pool.tensor_tensor(nxt[:, P:w], sp[0][:, P:2 * P], sp[0][:, 2 * P:3 * P], ALU.add).then_inc(b_carry, 1)
                else:
                    pool.wait_ge(b_carry, 3 * hd + j)
                    pool.tensor_copy(nxt[:, 0:P], sp[j][:, 0:P])
                    pool.tensor_tensor(nxt[:, P:w], sp[j][:, P:w], carry[j][:, :], ALU.add).then_inc(b_carry, 1)

        def act_b_stick(act, hd):
            for j in range(4):
                act.wait_ge(b_logs, 4 * hd + j + 1)
                if hd:
                    act.wait_ge(b_out, hd)
                act.activation(stick[j][:, :], z_bank[j], ACT.Exp).then_inc(b_stick, 1)

        def dve_b_mixed(dve, hd):
            dve.wait_ge(b_out, hd + 1)
            o = HEAD_DIM * (hd % 2)
            dve.tensor_copy(mixed[o:o + HEAD_DIM, QC + hd // 2, :], ps[0:HEAD_DIM, 4, :]).then_inc(b_mixed, 1)

        block = ctx.enter_context(nc.Block())

        @block.sync
        def _(sync):
            for t in range(TT):
                sync.dma_start(x_in[:, t, :], x[0, t * P:(t + 1) * P, :]).then_inc(x_loaded, 16)
            sync.dma_start(meta_in[:, :], meta_tokens).then_inc(meta_loaded, 16)
            load(sync, 0)
            load(sync, 1)
            with sync.Fori(1, FH) as it:
                load(sync, U_UP1, it)
                load(sync, U_UP1 + 1, it)
            with sync.Fori(0, DC // 2) as it:
                for k in range(4):
                    load(sync, U_DN1 + k, 2 * it)
            for n in range(U_IN, U_UP2):
                load(sync, n)
            with sync.Fori(0, FH) as it:
                load(sync, U_UP2, it)
                load(sync, U_UP2 + 1, it)
            with sync.Fori(0, DC // 2) as it:
                for k in range(4):
                    load(sync, U_DN2 + k, 2 * it)

        @block.gpsimd
        def _(pool):
            step = [0]

            def made(ins):
                step[0] += 1
                ins.then_inc(const_step, 1)
                pool.wait_ge(const_step, step[0])

            made(pool.memset(ones[:, :], 1.0))
            made(pool.memset(ident[:, :], 0.0))
            pool.affine_select(ident[:, :], ident[:, :], [[-1, P]], ALU.not_equal, 1.0, base=0,
                               channel_multiplier=1).then_inc(const_done, 1)
            for c in range(DC):
                finish_sum(pool, c, c % 2, T, first=c == 0)
            finish_sum(pool, DC, 0, T, first=True, taken=(mean_done, 1))
            for c in range(1, DC):
                finish_sum(pool, DC + c, c % 2, T)

            pool.wait_ge(acc_full, M_IN)
            made(pool.memset(head_ones[:, :], 0.0))
            for o in range(0, P, HEAD_DIM):
                made(pool.memset(head_ones[o:o + HEAD_DIM, o:o + HEAD_DIM], 1.0))
            pool.memset(neg_ones[:, :], -1.0)
            made(pool.memset(neg_tri[:, :], -1.0))
            made(pool.affine_select(neg_tri[:, :], neg_tri[:, :], [[-1, P]], ALU.is_ge, 0.0, base=0,
                                    channel_multiplier=1))
            made(pool.memset(causal[:, :], 1.0))
            made(pool.affine_select(causal[:, :], causal[:, :], [[1, P]], ALU.is_gt, 0.0, base=0,
                                    channel_multiplier=-1))
            made(pool.memset(future_bf[:, :], 0.0))
            made(pool.affine_select(future_bf[:, :], future_bf[:, :], [[1, P]], ALU.is_gt, -MASKED, base=0,
                                    channel_multiplier=-1))
            made(pool.tensor_copy(ident_bf[:, :], ident[:, :]))
            for t in range(TT):
                for lo, w, base in ((0, P, 0), (P, CHUNK, CHUNK), (P + CHUNK, N_META, N_META + t * P)):
                    last = pool.iota(dist[:, t, lo:lo + w], [[-1, w]], base=base, channel_multiplier=1,
                                     allow_small_or_imprecise_dtypes=True)
            last.then_inc(const_done, 1)
            for hd in range(B_HEADS):
                pool_b(pool, hd)
            for g, (c0, n) in enumerate(((0, QC), (QC, HC))):
                for k in range(n):
                    pool.wait_ge(on_sq, c0 + k + 1)
                    if k == 0:
                        pool.wait_ge(*((on_mean, g) if g else (mean_done, 2)))
                        pool.tensor_copy(sq_sum[:, 0:SEQ], tmp_a[0][:, 0:SEQ]).then_inc(on_added, 1)
                    else:
                        pool.wait_ge(on_added, c0 + k)
                        pool.tensor_tensor(sq_sum[:, 0:SEQ], sq_sum[:, 0:SEQ], tmp_a[k % 2][:, 0:SEQ],
                                           ALU.add).then_inc(on_added, 1)
            finish_sum(pool, 2 * DC, 0, SEQ, first=True, taken=(on_mean, 2))
            for c in range(1, DC):
                finish_sum(pool, 2 * DC + c, c % 2, SEQ)

        @block.tensor
        def _(pe):
            pe.wait_ge(const_done, 1)
            pe.wait_ge(small_loaded, SMALL)
            pe.transpose(ps[:, 7, 0:GAINS], gain_rows[:, :], ident[0:GAINS, 0:GAINS]).then_inc(gains_turned, 1)
            pe.wait_ge(x_loaded, 16 * TT)
            pe.wait_ge(meta_loaded, 16)
            for c in range(DC):
                if c == 3:
                    pe.wait_ge(gains_done, 1)
                if c >= 4:
                    pe.wait_ge(evacuated, c - 3)
                b = 2 * (c % 4)
                for t in range(TT):
                    pe.transpose(ps[:, b, t * P:(t + 1) * P], x_in[:, t, c * P:(c + 1) * P], ident[:, :])
                pe.transpose(ps[:, b + 1, 0:N_META], meta_in[:, c * P:(c + 1) * P],
                             ident[0:N_META, 0:N_META]).then_inc(acc_full, 1)
            pe_up(pe, U_UP1, M_UP1, T, x_hi, x_lo, 0)
            pe.wait_ge(g_lo_done, FC)
            with pe.Fori(0, DC // 2) as it:
                for k in range(2):
                    pe_down_chunk(pe, M_DN1 + 2 * k, U_DN1 + 2 * k, T, g1_hi, g1_lo, dm=it)

            for use, k in in_uses:
                m = m_in[use, k]
                if (use, k) == ("norm", 0):
                    norm_sum(pe, m, T, 2 * DC)
                elif use == "chunk":
                    pair_chunk(pe, m, U_IN + k // 2, k % 2, T, x_hi, x_lo, fresh=(x_lo_done, DC) if k == 0 else None)
                elif use == "qk":
                    pe.wait_ge(qk_squared, k + 1)
                    pe.wait_ge(const_done, 2)
                    pe.wait_ge(evacuated, m - 3)
                    for a in range(2):
                        last = pe.matmul(slot(m, T)[:, a, :], head_ones[:, :],
                                         tmp_a[k % 2][:, a * HALF:(a + 1) * HALF], start=True, stop=True)
                    last.then_inc(acc_full, 1)
                elif use == "v":
                    src = C_VA if k == 0 else C_VB + k - 1
                    pe.wait_ge(evacuated, max(m_in["chunk", src] + 1, m - 3))
                    b = 2 * (m % 4)
                    for t in range(TT):
                        pe.transpose(ps[:, b, t * P:(t + 1) * P], v_t[:, k, t * P:(t + 1) * P], ident[:, :])
                    pe.transpose(ps[0:N_META, b + 1, 0:P], v_t[:, k, SEQ:T], ident[:, :]).then_inc(acc_full, 1)

            pe.wait_ge(evacuated, M_OUT_NORM)
            pe.wait_ge(qk_done, QC + 2 * A_KV_HEADS)
            pe.wait_ge(v_edge_done, 1)
            for u in range(UNITS):
                pe_a_scores(pe, u)
                pe_b_scores(pe, u)
                if u:
                    pe_b_out(pe, u - 1)
                pe_a_turn(pe, u)
                pe_b_logs(pe, u)
                pe_a_out(pe, u)
            pe_b_out(pe, UNITS - 1)

            pe.wait_ge(a_mixed, UNITS)
            pe.wait_ge(b_mixed, UNITS)
            for g, n in enumerate((QC, QC + HC)):
                pe.wait_ge(on_added, n)
                pe.matmul(slot(M_OUT_NORM + g, SEQ), ones[:, :], sq_sum[:, 0:SEQ], start=True,
                          stop=True).then_inc(acc_full, 1)
            for d in range(DC):
                pair_chunk(pe, M_WO + d, U_WO + d // 2, d % 2, SEQ, mix_hi, mix_lo,
                           fresh=(on_lo, 0) if d == 0 else None)

            pe_up(pe, U_UP2, M_UP2, SEQ, x2_hi, x2_lo, 2 * DC)
            pe.wait_ge(g_lo_done, 2 * FC)

            def turn_out(par, d):
                pe.wait_ge(evacuated, 2 * d + M_DN2 + 2)
                if not isinstance(d, int) or d >= 2:
                    pe.wait_ge(out_staged, d - 1)
                b = 2 * ((M_DN2 + 2 * par + 1) % 4)
                for t in range(TT):
                    last = pe.transpose(ps[:, b, t * P:(t + 1) * P], tmp_b[par][:, t * P:(t + 1) * P], ident[:, :])
                last.then_inc(out_turned, 1)

            def down_out(k, it=0, turn=True):
                if turn:
                    turn_out(1 - k, 2 * it + k - 1)
                pe_down_chunk(pe, M_DN2 + 2 * k, U_DN2 + 2 * k, SEQ, g2_hi, g2_lo, dm=it)

            down_out(0, turn=False)
            down_out(1)
            with pe.Fori(1, DC // 2) as it:
                down_out(0, it)
                down_out(1, it)
            turn_out(1, DC - 1)

        @block.scalar
        def _(act):
            row = 0
            for src in (ffn1_norm_g, mix_norm_g, ffn2_norm_g, attn_out_g, sb_out_g):
                rows = src.shape[1] // P
                act.dma_start(gain_rows[row:row + rows, :],
                              src[0].rearrange("(c p) -> c p", p=P)).then_inc(small_loaded, 16)
                row += rows
            for k, src in enumerate((q_norm_g, k_norm_g)):
                for o in range(0, P, HEAD_DIM):
                    act.dma_start(gain_rows[row + k:row + k + 1, o:o + HEAD_DIM], src).then_inc(small_loaded, 16)
            act.dma_start(sink_col[:, :], sinks.to_broadcast([P, A_HEADS])).then_inc(small_loaded, 16)
            act.wait_ge(gains_done, 2)
            for c in range(DC):
                finish_hi(act, G_FFN1, c, c % 2, c, T, x_hi, M_X + c + 1)
            split_hi(act, 0)
            act_up(act, U_UP1, M_UP1, 0, T, g1_hi, 0)

            def down(k, it):
                split_hi(act, U_DN1 + 2 * k + 1, 2 * it, step=2)
                split_hi(act, U_DN1 + 2 * k + 2, 2 * it, step=2)
                finish_hi(act, G_MIX, 2 * it + DC + k, k, 2 * it + k, T, x_hi, 4 * it + M_DN1 + 2 * k + 2)

            with act.Fori(0, DC // 2 - 1) as it:
                down(0, it)
                down(1, it)
            down(0, DC // 2 - 1)
            down(1, DC // 2 - 1)

            for use, k in in_uses:
                m = m_in[use, k]
                if use == "chunk":
                    if k % 2 == 0:
                        split_hi(act, U_IN + k // 2 + 1)
                    if k == 0:
                        rms_act(act, T, 1)
                    if C_VA < k <= C_VA + QC + KC:
                        n = k - C_VA - 1
                        act.wait_ge(evacuated, m_in["chunk", n] + 1)
                        if n >= 2:
                            act.wait_ge(acc_full, m_in["qk", n - 2] + 1)
                        act.activation(tmp_a[n % 2][:, :], qa[:, n, :] if n < QC else k_a[:, :],
                                       ACT.Square).then_inc(qk_squared, 1)
                elif use == "qk":
                    act.wait_ge(qk_inv, k + 1)
                    act.activation(tmp_b[k % 2][:, :], tmp_b[k % 2][:, :], ACT.Sqrt).then_inc(qk_rms, 1)

            act.preload_act_table_set(LN_EXP)
            for u in range(UNITS):
                act_a_exp(act, u)
                act_b_ln(act, u)
                act_a_pt(act, u)
                act_b_stick(act, u)

            for g, (c0, n) in enumerate(((0, QC), (QC, HC))):
                act.wait_ge(*((b_mixed, UNITS) if g else (a_mixed, UNITS)))
                for k in range(n):
                    if c0 + k >= 2:
                        act.wait_ge(on_added, c0 + k - 1)
                    act.activation(tmp_a[k % 2][:, 0:SEQ], mixed[:, c0 + k, :], ACT.Square).then_inc(on_sq, 1)
            for g in range(2):
                act.wait_ge(on_inv, g + 1)
                act.activation(tmp_b[g][:, 0:SEQ], tmp_b[g][:, 0:SEQ], ACT.Sqrt).then_inc(on_rms, 1)
            for c in range(MC):
                act.wait_ge(on_scaled, c + 1)
                act.activation(mix_hi[:, c, :], mixed[:, c, :], ACT.Copy, scale=gains[:, G_OUT + c:G_OUT + c + 1]).then_inc(on_hi, 1)
            for d in range(DC):
                if d % 2 == 0:
                    split_hi(act, U_WO + d // 2 + 1)
                finish_hi(act, G_FFN2, 2 * DC + d, d % 2, d, SEQ, x2_hi, M_WO + d + 1)
            act_up(act, U_UP2, M_UP2, FC, SEQ, g2_hi, 2)

            def stage(par, d, uses):
                act.wait_ge(out_turned, d + 1)
                if not isinstance(d, int) or d >= 2:
                    act.wait_ge(out_written[par], uses)
                b = 2 * ((M_DN2 + 2 * par + 1) % 4)
                act.activation(tmp_a[par][:, 0:SEQ], ps[:, b, :], ACT.Copy).then_inc(out_staged, 1)
                act.wait_ge(out_staged, d + 1)
                act.dma_start(out[0].rearrange("(t p) n -> p t n", p=P)[:, :, bass.ds(d * P, P)],
                              tmp_a[par][:, 0:SEQ].rearrange("p (t n) -> p t n", n=P)).then_inc(out_written[par], 16)

            def down_out(k, it=0, out_chunk=True):
                split_hi(act, U_DN2 + 2 * k + 1, 2 * it, step=2)
                split_hi(act, U_DN2 + 2 * k + 2, 2 * it, step=2)
                if out_chunk:
                    stage(1 - k, 2 * it + k - 1, 16 * (it if k else it - 1))

            down_out(0, out_chunk=False)
            down_out(1)
            with act.Fori(1, DC // 2 - 1) as it:
                down_out(0, it)
                down_out(1, it)
            for k in range(2):
                d = DC - 2 + k
                split_hi(act, U_DN2 + 2 * d + 1)
                split_hi(act, U_DN2 + 2 * d + 2)
                stage(1 - k, d - 1, 16 * ((d - 1) // 2))
            stage(1, DC - 1, 16 * ((DC - 1) // 2))
            for s in range(2):
                act.wait_ge(out_written[s], 16 * DC // 2)

        @block.vector
        def _(dve):
            dve.wait_ge(gains_turned, 1)
            dve.tensor_copy(gains[:, :], ps[:, 7, 0:GAINS]).then_inc(gains_done, 1)
            dve.wait_ge(gains_done, 1)
            dve.tensor_scalar(head_gain[:, 0:1], head_gain[:, 0:1], SCALE, None, ALU.mult).then_inc(gains_done, 1)
            for c in range(DC + 1):
                if c < DC:
                    b = 2 * (c % 4)
                    dve.wait_ge(acc_full, M_X + c + 1)
                    dve.tensor_copy(h[:, c, 0:SEQ], ps[:, b, 0:SEQ])
                    dve.tensor_copy(h[:, c, SEQ:T], ps[:, b + 1, 0:N_META]).then_inc(evacuated, 1)
                if c:
                    finish_lo(dve, G_FFN1, c - 1, c - 1, T, x_hi, x_lo)
            split_lo(dve, 0)
            dve_up(dve, U_UP1, M_UP1, 0, T, g1_hi, g1_lo, 0)

            def add_chunk(m, d, cols, half, dm=0, uses=2, frees=2):
                dve.wait_ge(acc_full, 4 * dm + m + uses)
                row = tok(h, d, cols)
                dve.scalar_tensor_tensor(row, slot(m, cols), half, row, ALU.mult, ALU.add).then_inc(evacuated, frees)

            def down(k, it):
                split_lo(dve, U_DN1 + 2 * k + 1, 2 * it)
                split_lo(dve, U_DN1 + 2 * k + 2, 2 * it)
                add_chunk(M_DN1 + 2 * k, 2 * it + k, T, 0.5, dm=it)
                finish_lo(dve, G_MIX, 2 * it + DC + k, 2 * it + k, T, x_hi, x_lo)

            with dve.Fori(0, DC // 2 - 1) as it:
                down(0, it)
                down(1, it)
            down(0, DC // 2 - 1)
            down(1, DC // 2 - 1)

            def head_norm(k):
                dve.wait_ge(qk_rms, k + 1)
                row = qa[:, k, :] if k < QC else k_a[:, :]
                gain = head_gain[:, 0:1] if k < QC else head_gain[:, 1:2]
                dve.scalar_tensor_tensor(row, row, gain, tmp_b[k % 2][:, :], ALU.mult, ALU.mult).then_inc(qk_done, 1)

            dve.wait_ge(gains_done, 2)
            for use, k in in_uses:
                m = m_in[use, k]
                if use == "chunk":
                    if k % 2 == 0:
                        split_lo(dve, U_IN + k // 2 + 1)
                    if k == 0:
                        rms_dve(dve, m + 1, T, 1)
                        dve.wait_ge(rms_done, 2)
                    dve.wait_ge(acc_full, m + 1)
                    dst = (qa[:, k, :] if k < C_KA else k_a[:, :] if k < C_VA else v_t[:, 0, :] if k < C_QB else
                           qb[:, k - C_QB, :] if k < C_KB else kb[:, k - C_KB, :] if k < C_VB else
                           v_t[:, 1 + k - C_VB, :])
                    dve.scalar_tensor_tensor(wide(dst, T), slot(m, T), SCALE if C_QB <= k < C_KB else 1.0,
                                             wide(rms_inv[:, :], T), ALU.mult,
                                             ALU.mult).then_inc(evacuated, 3 if k == 0 else 1)
                elif use == "qk":
                    dve.wait_ge(acc_full, m + 1)
                    if k >= 1:
                        head_norm(k - 1)
                    dve.tensor_scalar(wide(tmp_b[k % 2][:, :], T), slot(m, T), 1.0 / HEAD_DIM, EPS, ALU.mult,
                                      ALU.add).then_inc(evacuated, 1)
                    dve.wait_ge(evacuated, m + 1)
                    dve.reciprocal(tmp_b[k % 2][:, :], tmp_b[k % 2][:, :]).then_inc(qk_inv, 1)
                elif use == "v":
                    if k == 0:
                        head_norm(QC)
                        dve.wait_ge(qk_done, QC + 1)
                        for g in range(A_KV_HEADS):
                            for e in range(2):
                                dve.tensor_copy(k_dup[g][e * HEAD_DIM:(e + 1) * HEAD_DIM, :],
                                                k_a[g * HEAD_DIM:(g + 1) * HEAD_DIM, :]).then_inc(qk_done, 1)
                    dve.wait_ge(acc_full, m + 1)
                    b = 2 * (m % 4)
                    dve.tensor_copy(v_nat[:, k, :, :].rearrange("p t n -> p (t n)"), ps[:, b, :])
                    dve.tensor_copy(v_meta[:, k, :], ps[0:N_META, b + 1, 0:P]).then_inc(evacuated, 1)
                    if k == 0:
                        dve.wait_ge(evacuated, m + 1)
                        dve.tensor_copy(v_edge[0:HEAD_DIM, 0, :], v_nat[0:HEAD_DIM, 0, 0, :])
                        dve.tensor_copy(v_edge[0:HEAD_DIM, 1:TT, :], v_nat[HEAD_DIM:P, 0, 0:TT - 1, :])
                        for t in range(TT):
                            last = dve.tensor_copy(v_edge[HEAD_DIM:EDGE, t, :], v_meta[:, 0, :])
                        last.then_inc(v_edge_done, 1)

            dve.wait_ge(const_done, 2)
            dve.scalar_tensor_tensor(dist[:, :, :], dist[:, :, :], -1.0, dist[:, :, :], ALU.mult,
                                     ALU.max).then_inc(dist_done, 1)
            dve.wait_ge(dist_done, 1)
            dve.memset(dist[0:CHUNK, :, CHUNK:P], MASKED)
            dve.memset(dist[CHUNK:P, :, P:P + CHUNK], MASKED)
            dve.memset(dist[0:CHUNK, 0, P:P + CHUNK], MASKED).then_inc(dist_done, 1)
            dve.wait_ge(dist_done, 2)
            for u in range(UNITS):
                dve_a_max(dve, u)
                dve_a_probs(dve, u)
                dve_b_soft(dve, u)
                if u:
                    dve_b_mixed(dve, u - 1)
                dve_a_mixed(dve, u)
            dve_b_mixed(dve, UNITS - 1)

            for g in range(2):
                m = M_OUT_NORM + g
                dve.wait_ge(acc_full, m + 1)
                dve.tensor_scalar(tmp_b[g][:, 0:SEQ], slot(m, SEQ), 1.0 / A_Q, EPS, ALU.mult,
                                  ALU.add).then_inc(on_mean, 1)
                dve.wait_ge(on_mean, g + 1)
                dve.reciprocal(tmp_b[g][:, 0:SEQ], tmp_b[g][:, 0:SEQ]).then_inc(on_inv, 1)
            for c in range(MC + 1):
                if c < MC:
                    dve.wait_ge(on_rms, c // QC + 1)
                    dve.tensor_tensor(mixed[:, c, :], mixed[:, c, :], tmp_b[c // QC][:, 0:SEQ], ALU.mult).then_inc(on_scaled, 1)
                if c:
                    dve.wait_ge(on_hi, c)
                    dve.wait_ge(on_scaled, c)
                    dve.scalar_tensor_tensor(mix_lo[:, c - 1, :], mixed[:, c - 1, :],
                                             gains[:, G_OUT + c - 1:G_OUT + c], mix_hi[:, c - 1, :].bitcast(F32),
                                             ALU.mult, ALU.subtract).then_inc(on_lo, 1)
            for d in range(DC):
                if d % 2 == 0:
                    split_lo(dve, U_WO + d // 2 + 1)
                add_chunk(M_WO + d, d, SEQ, 1.0, uses=1, frees=1 if d else 3)
                finish_lo(dve, G_FFN2, 2 * DC + d, d, SEQ, x2_hi, x2_lo)
            dve_up(dve, U_UP2, M_UP2, FC, SEQ, g2_hi, g2_lo, 2)

            def down_out(k, it):
                split_lo(dve, U_DN2 + 2 * k + 1, 2 * it)
                split_lo(dve, U_DN2 + 2 * k + 2, 2 * it)
                m, d = M_DN2 + 2 * k, 2 * it + k
                dve.wait_ge(acc_full, 4 * it + m + 2)
                if not isinstance(it, int) or it:
                    dve.wait_ge(out_turned, d - 1)
                dve.scalar_tensor_tensor(tmp_b[k][:, 0:SEQ], slot(m, SEQ), 0.5, tok(h, d, SEQ), ALU.mult,
                                         ALU.add).then_inc(evacuated, 2)

            down_out(0, 0)
            down_out(1, 0)
            with dve.Fori(1, DC // 2 - 1) as it:
                down_out(0, it)
                down_out(1, it)
            down_out(0, DC // 2 - 1)
            down_out(1, DC // 2 - 1)


_INS = ["x", "meta_tokens", "ffn1_norm_g", "ffn1_w_gate", "ffn1_w_up", "ffn1_w_down", "mix_norm_g", "w_in",
        "q_norm_g", "k_norm_g", "sinks", "attn_out_g", "sb_out_g", "w_o",
        "ffn2_norm_g", "ffn2_w_gate", "ffn2_w_up", "ffn2_w_down"]


def kernel(**inputs):
    import numpy as _np
    import concourse.bacc as _bacc
    from concourse import mybir as _mybir
    from concourse.bass_utils import run_bass_kernel_spmd as _run

    nc = _bacc.Bacc("TRN2", target_bir_lowering=False, num_devices=1)
    arrays, args = {}, []
    for name in _INS:
        a = _np.ascontiguousarray(inputs[name])
        arrays[f"in_{name}_dram"] = a
        args.append(nc.dram_tensor(f"in_{name}_dram", a.shape, _mybir.dt.from_np(a.dtype), kind="ExternalInput").ap())
    shape = tuple(inputs["x"].shape)
    out = nc.dram_tensor("out_0_dram", shape, _mybir.dt.from_np(_np.dtype("float32")), kind="ExternalOutput").ap()
    hybrid_layer_kernel(nc, *args, out)
    r = _run(nc, [arrays], core_ids=[0])
    return r.results[0]["out_0_dram"]
```

```python
from contextlib import ExitStack

import concourse.bass as bass
from concourse import mybir

ALU = mybir.AluOpType
ACT = mybir.ActivationFunctionType
AX = mybir.AxisListType
F32 = mybir.dt.float32
F32R = mybir.dt.float32r
BF16 = mybir.dt.bfloat16

P = 128
BANK = 512
HEAD_DIM = 64
CHUNK = 64
EPS = 1e-6
MASKED = 3e38
LN_EXP = "natural_log_exp_and_others"


def hybrid_layer_kernel(nc, x, meta_tokens, ffn1_norm_g, ffn1_w_gate, ffn1_w_up, ffn1_w_down, mix_norm_g, w_in,
                        q_norm_g, k_norm_g, sinks, attn_out_g, sb_out_g, w_o,
                        ffn2_norm_g, ffn2_w_gate, ffn2_w_up, ffn2_w_down, out):
    _, SEQ, D = x.shape
    N_META = meta_tokens.shape[0]
    T = SEQ + N_META
    HALF = T // 2
    F = ffn1_w_gate.shape[2]
    DC, FC = D // P, F // P
    TT = SEQ // P
    A_HEADS = sinks.shape[1]
    D_MIX = w_o.shape[1]
    B_HEADS = sb_out_g.shape[1] // HEAD_DIM
    A_Q = A_HEADS * HEAD_DIM
    D_IN = w_in.shape[2]
    B_W = B_HEADS * HEAD_DIM
    A_KV = (D_IN - A_Q - 3 * B_W) // 2
    A_KV_HEADS = A_KV // HEAD_DIM
    GROUP = A_HEADS // A_KV_HEADS
    QC, KC = A_Q // P, A_KV // P
    HC = B_W // P
    MC = D_MIX // P
    SCALE = HEAD_DIM ** -0.5
    assert (D, F, T, A_KV, GROUP, N_META) == (1024, 2816, 528, P, 4, 16) and FC % 2 == 0


    PAIR = 2 * DC * P
    FH = FC // 2
    DOWN = FH * P
    U_UP1 = 0
    U_DN1 = U_UP1 + FC
    U_IN = U_DN1 + 2 * DC
    U_WO = U_IN + D_IN // (2 * P)
    U_UP2 = U_WO + D // (2 * P)
    U_DN2 = U_UP2 + FC
    U_END = U_DN2 + 2 * DC

    def unit_size(n):
        return DOWN if U_DN1 <= n < U_IN or n >= U_DN2 else PAIR

    IN_CHUNKS = D_IN // P
    V_CHUNKS = KC + HC
    M_X = 0
    M_UP1 = M_X + DC
    M_DN1 = M_UP1 + 2 * FC + 2
    M_IN = M_DN1 + 2 * DC
    C_KA, C_VA, C_QB, C_KB, C_VB = QC, QC + KC, QC + 2 * KC, QC + 2 * KC + HC, QC + 2 * KC + 2 * HC
    in_uses = [("chunk", 0), ("norm", 0), ("norm", 1)]
    for c in range(1, IN_CHUNKS):
        in_uses.append(("chunk", c))
        if c % 2 and QC < c <= QC + 2 * (QC + KC):
            in_uses.append(("qk", (c - QC) // 2))
        if c == C_VB:
            in_uses.append(("v", 0))
        elif c > C_VB:
            in_uses.append(("v", c - C_VB))
    in_uses.append(("v", HC))
    m_in = {use: M_IN + k for k, use in enumerate(in_uses)}
    M_HEADS = M_IN + len(in_uses)
    M_WO = M_HEADS + (3 - M_HEADS) % 4
    M_UP2 = M_WO + DC
    M_DN2 = M_UP2 + 2 * FC + 2

    EDGE = CHUNK + N_META
    A_KEYS = P + EDGE
    B_TILES = 3
    B_COLS = [2 * P + P, 3 * P, 4 * P]
    B_PARTS = [[(2, 0), (3, 2 * P)], [(1, 0)], [(0, 0)]]
    UNITS = TT * A_KV_HEADS
    assert UNITS == B_HEADS and TT == 4 and B_HEADS * N_META == P

    with ExitStack() as ctx:
        def sb(name, shape, dt=F32, side="left", into=None):
            return (into or ctx).enter_context(nc.sbuf_tensor(name, shape, dt, side=side))

        def sem(name):
            return ctx.enter_context(nc.semaphore(name))

        raw = [sb(f"raw{s}", [P, PAIR]) for s in range(2)]
        w_hi = [sb(f"w_hi{s}", [P, PAIR], F32R) for s in range(2)]
        w_lo = [sb(f"w_lo{s}", [P, PAIR], F32R) for s in range(2)]
        h = sb("h", [P, DC, T])
        rms_inv = sb("rms_inv", [P, T])
        sq_sum = sb("sq_sum", [P, T])
        tmp_a = [sb(f"tmp_a{s}", [P, T]) for s in range(2)]
        tmp_b = [sb(f"tmp_b{s}", [P, T]) for s in range(2)]
        ident = sb("ident", [P, P])
        ones = sb("ones", [P, P])
        G_FFN1, G_MIX, G_FFN2, G_OUT = 0, DC, 2 * DC, 3 * DC
        GAINS = 3 * DC + MC + 2
        gain_rows = sb("gain_rows", [GAINS, P])
        gains = sb("gains", [P, GAINS])
        head_gain = gains[:, GAINS - 2:GAINS]
        sink_col = sb("sink_col", [P, A_HEADS])

        right, left = ExitStack(), ExitStack()
        x_hi = sb("x_hi", [P, DC, T], F32R, "right", right)
        x_lo = sb("x_lo", [P, DC, T], F32R, "right", right)
        x_in = sb("x_in", [P, TT, D], into=left)
        meta_in = sb("meta_in", [N_META, D], into=left)
        left.close()
        left = ExitStack()
        g1_hi = sb("g1_hi", [P, FC, T], F32R, into=left)
        g1_lo = sb("g1_lo", [P, FC, T], F32R, into=left)
        left.close()
        left, early, late = ExitStack(), ExitStack(), ExitStack()
        qa = sb("qa", [P, QC, SEQ], into=left)
        k_win = sb("k_win", [P, A_KV_HEADS, TT, A_KEYS], into=left)
        qb = sb("qb", [P, HC, SEQ], into=left)
        kb = sb("kb", [P, HC, T], into=left)
        v_nat = sb("v_nat", [P, V_CHUNKS, TT, P], into=left)
        v_edge = sb("v_edge", [EDGE, TT, P], into=left)
        k_meta = sb("k_meta", [P, HC, P], into=left)
        v_meta = sb("v_meta", [P, HC, P], into=left)
        row_max = sb("row_max", [P, GROUP], into=left)
        neg_max = sb("neg_max", [P, GROUP], into=left)
        sink_exp = sb("sink_exp", [P, GROUP], into=left)
        row_sum = sb("row_sum", [P, GROUP], into=left)
        neg_ones = sb("neg_ones", [P, P], into=left)
        neg_tri = sb("neg_tri", [P, P], into=left)
        neg_tri_meta = sb("neg_tri_meta", [P, P], into=left)
        neg_sel = sb("neg_sel", [P, 2 * P - N_META], into=left)
        causal = sb("causal", [P, P], into=left)
        ident_bf = sb("ident_bf", [P, P], BF16, into=left)
        future_bf = sb("future_bf", [P, P], BF16, into=left)
        dist = sb("dist", [P, TT, A_KEYS], into=left)
        k_a = sb("k_a", [P, T], into=early)
        v_t = sb("v_t", [P, V_CHUNKS, T], into=early)
        v_pad = sb("v_pad", [P, HC, P], into=early)
        va_meta = sb("va_meta", [N_META, P], into=early)
        head_ones = sb("head_ones", [P, P], into=early)
        early.close()
        mix_hi = sb("mix_hi", [P, MC, SEQ], F32R, into=late)
        mix_lo = sb("mix_lo", [P, MC, SEQ], F32R, into=late)
        right.close()
        right = ExitStack()
        mixed = sb("mixed", [P, MC, SEQ], side="right", into=right)
        sp = [sb(f"sp{j}", [P, B_COLS[j]], side="right", into=right) for j in range(B_TILES)]
        stick = [sb(f"stick{j}", [P, B_COLS[j]], side="right", into=right) for j in range(B_TILES)]
        sp_meta = sb("sp_meta", [P, SEQ], side="right", into=right)
        stick_meta = sb("stick_meta", [P, SEQ], side="right", into=right)
        carry = [None] + [sb(f"carry{j}", [P, j * P + P], side="right", into=right) for j in range(1, 4)]
        probs = sb("probs", [P, GROUP, A_KEYS], side="right", into=right)
        p_own = sb("p_own", [P, GROUP, P], side="right", into=right)
        p_edge = sb("p_edge", [EDGE, GROUP, P], side="right", into=right)
        right.close()
        late.close()
        left.close()
        left, right = ExitStack(), ExitStack()
        g2_hi = sb("g2_hi", [P, FC, SEQ], F32R, into=left)
        g2_lo = sb("g2_lo", [P, FC, SEQ], F32R, into=left)
        x2_hi = sb("x2_hi", [P, DC, SEQ], F32R, "right", right)
        x2_lo = sb("x2_lo", [P, DC, SEQ], F32R, "right", right)
        left.close()
        right.close()

        ps = ctx.enter_context(nc.psum_tensor("ps", [P, 8, BANK], F32))
        z_tile = [ps[:, 2 * j, 0:B_COLS[j]] for j in range(B_TILES)]
        OUT_BANK, META_BANK = 1, 3
        A_BANKS = (6, 7)
        A_OUT_BANK = 5
        META_OUT_BANKS = (7, 5, 3, 1)
        NORM_BANKS = (5, 7)

        def slot(m, cols):
            b = 2 * (m % 4)
            return ps[:, b, 0:SEQ] if cols == SEQ else ps[:, b:b + 2, 0:HALF]

        def wide(ap, cols):
            return ap if cols == SEQ else ap.rearrange("p (a b) -> p a b", b=HALF)

        def tok(t, c, cols):
            row = t[:, bass.ds(c, 1), 0:cols].rearrange("p a b -> p (a b)")
            return wide(row, cols)

        raw_loaded = [sem(f"raw_loaded{s}") for s in range(2)]
        hi_split, lo_split = sem("hi_split"), sem("lo_split")
        acc_full, evacuated = sem("acc_full"), sem("evacuated")
        x_loaded = [sem(f"x_loaded{q}") for q in range(4)]
        meta_loaded, small_loaded = sem("meta_loaded"), sem("small_loaded")
        gate0_loaded, gate0_hi, gate0_lo = sem("gate0_loaded"), sem("gate0_hi"), sem("gate0_lo")
        const_step, const_done = sem("const_step"), sem("const_done")
        x_hi_done, x_lo_done = sem("x_hi_done"), sem("x_lo_done")
        sq_made, sq_done, sq_added = sem("sq_made"), sem("sq_done"), sem("sq_added")
        mean_done, inv_done, rms_done = sem("mean_done"), sem("inv_done"), sem("rms_done")
        silu_done, hidden_done, g_hi_done, g_lo_done = (
            sem(k) for k in ("silu_done", "hidden_done", "g_hi_done", "g_lo_done"))
        v_edge_done = sem("v_edge_done")
        qk_squared, qk_mean, qk_inv, qk_rms, qk_scaled, qk_done = (
            sem(k) for k in ("qk_squared", "qk_mean", "qk_inv", "qk_rms", "qk_scaled", "qk_done"))
        a_scores, a_biased, a_max, a_sink_max, a_neg = (sem(k) for k in ("a_scores", "a_biased", "a_max",
                                                                        "a_sink_max", "a_neg"))
        a_sink_in, a_exp, a_total, a_inv, a_probs = (sem(k) for k in ("a_sink_in", "a_exp", "a_total", "a_inv",
                                                                     "a_probs"))
        a_turned, a_pt, a_out, a_mixed = (sem(k) for k in ("a_turned", "a_pt", "a_out", "a_mixed"))
        b_scores, b_abs, b_exp, b_ln, b_soft = (sem(k) for k in ("b_scores", "b_abs", "b_exp", "b_ln", "b_soft"))
        b_masked, b_carry, b_logs, b_stick, b_out, b_mixed = (
            sem(k) for k in ("b_masked", "b_carry", "b_logs", "b_stick", "b_out", "b_mixed"))
        k_win_done, meta_padded = sem("k_win_done"), sem("meta_padded")
        m_scores, m_abs, m_exp, m_ln, m_soft, m_summed, m_stick, m_out, m_added = (
            sem(k) for k in ("m_scores", "m_abs", "m_exp", "m_ln", "m_soft", "m_summed", "m_stick", "m_out",
                             "m_added"))
        on_sq, on_added, on_sum, on_mean, on_inv, on_rms, on_scaled, on_hi, on_lo = (
            sem(k) for k in ("on_sq", "on_added", "on_sum", "on_mean", "on_inv", "on_rms", "on_scaled", "on_hi",
                             "on_lo"))
        out_turned, out_staged = sem("out_turned"), sem("out_staged")
        gains_turned, gains_done, dist_done = sem("gains_turned"), sem("gains_done"), sem("dist_done")
        SMALL = 16 * 10
        out_written = [sem(f"out_written{s}") for s in range(2)]

        def full_after(n):
            for base, m in ((U_DN2, M_DN2), (U_UP2, M_UP2), (U_WO, M_WO), (U_IN, M_IN), (U_DN1, M_DN1),
                            (U_UP1, M_UP1)):
                if n >= base:
                    k = n - base
                    if base == U_IN:
                        return m_in["chunk", 2 * k + 1] + 1
                    return m + {U_DN1: k + 1, U_DN2: k + 1, U_WO: 2 * k + 2}.get(base, 2 * k + 4)

        def pair_src(n0, dy):
            r = raw[n0 % 2]
            pair = r.rearrange("p (c w o) -> p c w o", c=DC, w=2)
            for base, w_gate, w_up in ((U_UP1, ffn1_w_gate, ffn1_w_up), (U_UP2, ffn2_w_gate, ffn2_w_up)):
                if base <= n0 < base + FC:
                    cols = bass.ds((n0 - base + 2 * dy) * P, P)
                    return [(pair[:, :, w, :], src[0].rearrange("(c p) n -> p c n", p=P)[:, :, cols])
                            for w, src in enumerate((w_gate, w_up))]
            src, base = (w_in, U_IN) if n0 < U_WO else (w_o, U_WO)
            cols = bass.ds((n0 - base + 2 * dy) * 2 * P, 2 * P)
            view = src[0].rearrange("(c p) n -> p c n", p=P)[:, :, cols]
            whole = r.rearrange("p (c n) -> p c n", c=DC)
            return [(whole[:, q * DC // 2:(q + 1) * DC // 2, :], view[:, q * DC // 2:(q + 1) * DC // 2, :])
                    for q in range(2)]

        def down_src(n0, dy):
            base, src = (U_DN1, ffn1_w_down) if n0 < U_IN else (U_DN2, ffn2_w_down)
            half = (n0 - base) % 2
            cols = bass.ds(((n0 - base) // 2 + dy) * P, P)
            view = src[0].rearrange("(c p) n -> p c n", p=P)[:, half * FH:(half + 1) * FH, cols]
            r = raw[n0 % 2][:, 0:DOWN].rearrange("p (c n) -> p c n", c=FH)
            return [(r[:, a:b, :], view[:, a:b, :]) for a, b in ((0, 6), (6, FH))]

        def placed(n0, dy):
            return (n0 + 2 * dy, 0) if isinstance(dy, int) else (n0, dy)

        def load(sync, n0, dy=0):
            if n0 >= 2 or not isinstance(dy, int):
                sync.wait_ge(lo_split, n0 - 1 + 2 * dy)
            for dst, src in (pair_src(n0, dy) if unit_size(n0) == PAIR else down_src(n0, dy)):
                sync.dma_start(dst, src).then_inc(raw_loaded[n0 % 2], 16)

        def split_hi(act, n0, dy=0, step=4):
            n0, dy = placed(n0, dy)
            if n0 >= U_END:
                return
            s, size = n0 % 2, unit_size(n0)
            act.wait_ge(raw_loaded[s], 32 * (n0 // 2 + 1) + 32 * dy)
            if not isinstance(dy, int):
                act.wait_ge(acc_full, full_after(n0) - step + step * dy)
            elif n0 >= 2:
                act.wait_ge(acc_full, full_after(n0 - 2))
            act.activation(w_hi[s][:, 0:size], raw[s][:, 0:size], ACT.Copy).then_inc(hi_split, 1)

        def split_lo(dve, n0, dy=0):
            n0, dy = placed(n0, dy)
            if n0 >= U_END:
                return
            s, size = n0 % 2, unit_size(n0)
            dve.wait_ge(hi_split, n0 + 1 + 2 * dy)
            dve.tensor_tensor(w_lo[s][:, 0:size], raw[s][:, 0:size], w_hi[s][:, 0:size].bitcast(F32),
                              ALU.subtract).then_inc(lo_split, 1)

        def passes(pe, m, cols, left_hi, left_lo, right_hi, right_lo, start, stop):
            dst = slot(m, cols)
            parts = [(dst, slice(0, SEQ))] if cols == SEQ else [
                (dst[:, a, :], slice(a * HALF, (a + 1) * HALF)) for a in range(2)]
            trio = ((left_hi, right_hi), (left_hi, right_lo), (left_lo, right_hi))
            for k, (lt, rt) in enumerate(trio):
                for o, r in parts:
                    last = pe.matmul(o, lt, rt[:, r], start=start and k == 0, stop=stop and k == 2)
            return last

        def pair_chunk(pe, m, n0, which, cols, rh, rl, dm=0, dy=0, fresh=None, part=None, skipped=0):
            s = n0 % 2
            very_first = n0 == 0 and isinstance(dy, int)
            if very_first and which == 0:
                pe.wait_ge(gate0_lo, 1)
            elif which == 0 or very_first:
                pe.wait_ge(lo_split, n0 + 1 + 2 * dy)
            if part is None:
                pe.wait_ge(evacuated, m - 3 + 4 * dm)
            whi = w_hi[s].rearrange("p (c w o) -> p c w o", c=DC, w=2)
            wlo = w_lo[s].rearrange("p (c w o) -> p c w o", c=DC, w=2)
            for c in part or range(DC):
                if fresh is not None:
                    pe.wait_ge(fresh[0], fresh[1] + c + 1)
                last = passes(pe, m, cols, whi[:, c, which, :], wlo[:, c, which, :], rh[:, c, :], rl[:, c, :],
                              c == 0, c == DC - 1)
            if c == DC - 1:
                last.then_inc(acc_full, 1 + skipped)

        def in_cols(k):
            return SEQ if k < C_KA or C_QB <= k < C_KB else T

        def norm_sum(pe, m, cols, sums):
            pe.wait_ge(sq_added, sums)
            pe.wait_ge(evacuated, m - 2)
            dst = slot(m, cols)
            if cols == SEQ:
                last = pe.matmul(dst, ones[:, :], sq_sum[:, 0:SEQ], start=True, stop=True)
            else:
                for a in range(2):
                    last = pe.matmul(dst[:, a, :], ones[:, :], sq_sum[:, a * HALF:(a + 1) * HALF],
                                     start=True, stop=True)
            last.then_inc(acc_full, 2)

        def pe_first_unit(pe, n0, m0, cols, rh, rl, done):
            pair_chunk(pe, m0, n0, 0, cols, rh, rl, fresh=(x_lo_done, done))
            norm_sum(pe, m0 + 1, cols, done + DC)
            pair_chunk(pe, m0 + 3, n0, 1, cols, rh, rl)

        def pe_up(pe, n0, m0, cols, rh, rl, done):
            pe_first_unit(pe, n0, m0, cols, rh, rl, done)
            for w in range(2):
                pair_chunk(pe, m0 + 4 + w, n0 + 1, w, cols, rh, rl)
            with pe.Fori(1, FH) as it:
                for k in range(2):
                    for w in range(2):
                        pair_chunk(pe, m0 + 2 + 2 * k + w, n0 + k, w, cols, rh, rl, dm=it, dy=it)

        def pe_down_chunk(pe, m, n0, cols, gh, gl, hidden0, dm=0, between=None):
            for half in range(2):
                s = (n0 + half) % 2
                pe.wait_ge(lo_split, n0 + half + 1 + 4 * dm)
                if half == 0:
                    pe.wait_ge(evacuated, m - 3 + 4 * dm)
                    pe.wait_ge(g_lo_done, hidden0 + FC - 1)
                for c in range(FH):
                    f = half * FH + c
                    if f == FC - 1:
                        pe.wait_ge(g_lo_done, hidden0 + FC)
                    last = passes(pe, m, cols, w_hi[s][:, c * P:(c + 1) * P], w_lo[s][:, c * P:(c + 1) * P],
                                  gh[:, f, :], gl[:, f, :], f == 0, f == FC - 1)
                last.then_inc(acc_full, 1)
                if half == 0 and between:
                    between()

        def finish_hi(act, g0, n, par, c, cols, xh, ready, squares=True):
            if squares:
                act.wait_ge(sq_added, n - 1)
            act.wait_ge(evacuated, ready)
            act.activation(tok(xh, c, cols), tok(h, c, cols), ACT.Copy,
                           scale=gains[:, bass.ds(c + g0, 1)]).then_inc(x_hi_done, 1)
            if squares:
                act.activation(wide(tmp_a[par][:, 0:cols], cols), tok(h, c, cols), ACT.Square).then_inc(sq_done, 1)

        def finish_lo(dve, g0, n, c, cols, xh, xl):
            dve.wait_ge(x_hi_done, n + 1)
            dve.scalar_tensor_tensor(tok(xl, c, cols), tok(h, c, cols), gains[:, bass.ds(c + g0, 1)],
                                     tok(xh, c, cols).bitcast(F32), ALU.mult, ALU.subtract).then_inc(x_lo_done, 1)

        def finish_sum(pool, n, par, cols, first=False, taken=None):
            pool.wait_ge(sq_done, n + 1 - DC)
            if first:
                if taken:
                    pool.wait_ge(*taken)
                pool.tensor_copy(sq_sum[:, 0:cols], tmp_a[par][:, 0:cols]).then_inc(sq_added, 1)
            else:
                pool.wait_ge(sq_added, n)
                pool.tensor_tensor(sq_sum[:, 0:cols], sq_sum[:, 0:cols], tmp_a[par][:, 0:cols],
                                   ALU.add).then_inc(sq_added, 1)

        def rms_dve(dve, m, cols, k):
            dve.wait_ge(acc_full, m + 1)
            dve.tensor_scalar(wide(rms_inv[:, 0:cols], cols), slot(m, cols), 1.0 / D, EPS,
                              ALU.mult, ALU.add).then_inc(mean_done, 1)
            dve.wait_ge(mean_done, k + 1)
            dve.reciprocal(rms_inv[:, 0:cols], rms_inv[:, 0:cols]).then_inc(inv_done, 1)

        def rms_act(act, cols, k):
            act.wait_ge(inv_done, k + 1)
            act.activation(rms_inv[:, 0:cols], rms_inv[:, 0:cols], ACT.Sqrt).then_inc(rms_done, 1)

        def scale_gate(dve, m, par, cols, dm=0, frees=1):
            dve.wait_ge(acc_full, m + 1 + 4 * dm)
            dve.tensor_tensor(wide(tmp_a[par][:, 0:cols], cols), slot(m, cols), wide(rms_inv[:, 0:cols], cols),
                              ALU.mult).then_inc(evacuated, frees)

        def scale_up(dve, m, par, cols, dm=0):
            dve.wait_ge(acc_full, m + 1 + 4 * dm)
            dve.tensor_tensor(wide(tmp_b[par][:, 0:cols], cols), slot(m, cols), wide(rms_inv[:, 0:cols], cols),
                              ALU.mult).then_inc(evacuated, 1)

        def hidden(dve, f0, m, k0, cols, dm=0, dk=0):
            par = k0 % 2
            dve.wait_ge(silu_done, f0 + k0 + 1 + 2 * dk)
            dve.wait_ge(evacuated, m + 1 + 4 * dm)
            dve.tensor_tensor(tmp_b[par][:, 0:cols], tmp_a[par][:, 0:cols], tmp_b[par][:, 0:cols],
                              ALU.mult).then_inc(hidden_done, 1)

        def hidden_lo(dve, f0, k0, cols, gh, gl, dk=0):
            dve.wait_ge(g_hi_done, f0 + k0 + 1 + 2 * dk)
            dve.tensor_tensor(gl[:, bass.ds(k0 + 2 * dk, 1), 0:cols].rearrange("p a b -> p (a b)"),
                              tmp_b[k0 % 2][:, 0:cols],
                              gh[:, bass.ds(k0 + 2 * dk, 1), 0:cols].rearrange("p a b -> p (a b)").bitcast(F32),
                              ALU.subtract).then_inc(g_lo_done, 1)

        def act_hidden(act, f0, m, k0, cols, gh, dm=0, dk=0):
            par = k0 % 2
            act.wait_ge(evacuated, m + 1 + 4 * dm)
            act.activation(tmp_a[par][:, 0:cols], tmp_a[par][:, 0:cols], ACT.Silu).then_inc(silu_done, 1)
            act.wait_ge(hidden_done, f0 + k0 + 1 + 2 * dk)
            act.activation(gh[:, bass.ds(k0 + 2 * dk, 1), 0:cols].rearrange("p a b -> p (a b)"),
                           tmp_b[par][:, 0:cols], ACT.Copy).then_inc(g_hi_done, 1)

        def act_up(act, n0, m0, f0, cols, gh, norm):
            def unit(k, dy=0):
                split_hi(act, n0 + k + 1, dy)
                act_hidden(act, f0, m0 + 2 + 2 * k, k, cols, gh, dm=dy, dk=dy)

            split_hi(act, n0 + 1)
            rms_act(act, cols, norm)
            act.preload_act_table_set("silu_and_others")
            act_hidden(act, f0, m0, 0, cols, gh)
            unit(1)
            with act.Fori(1, FH - 1) as it:
                unit(0, it)
                unit(1, it)
            unit(FC - 2)
            unit(FC - 1)

        def dve_up(dve, n0, m0, f0, cols, gh, gl, norm):
            def unit(k, dy=0):
                m = m0 + 2 + 2 * k
                split_lo(dve, n0 + k + 1, dy)
                scale_gate(dve, m, k % 2, cols, dm=dy)
                if k:
                    hidden_lo(dve, f0, k - 1, cols, gh, gl, dk=dy)
                else:
                    hidden_lo(dve, f0, 1, cols, gh, gl, dk=dy - 1)
                scale_up(dve, m + 1, k % 2, cols, dm=dy)
                hidden(dve, f0, m + 1, k, cols, dm=dy, dk=dy)

            split_lo(dve, n0 + 1)
            rms_dve(dve, m0 + 1, cols, norm)
            dve.wait_ge(rms_done, norm + 1)
            scale_gate(dve, m0, 0, cols, frees=3)
            scale_up(dve, m0 + 3, 0, cols)
            hidden(dve, f0, m0 + 3, 0, cols)
            unit(1)
            with dve.Fori(1, FH - 1) as it:
                unit(0, it)
                unit(1, it)
            unit(FC - 2)
            unit(FC - 1)
            hidden_lo(dve, f0, FC - 1, cols, gh, gl)

        def a_heads(u):
            for r in range(GROUP):
                hd = GROUP * (u % A_KV_HEADS) + r
                yield r, hd, hd // 2, HEAD_DIM * (hd % 2)

        def pe_a_scores(pe, u):
            t = u // A_KV_HEADS
            if u:
                pe.wait_ge(a_pt, 2 * u)
            for r, hd, c, o in sorted(a_heads(u), key=lambda head: head[3]):
                at = A_KEYS * (r // 2)
                last = pe.matmul(ps[:, A_BANKS[r % 2], at:at + A_KEYS], qa[o:o + HEAD_DIM, c, t * P:(t + 1) * P],
                                 k_win[o:o + HEAD_DIM, u % A_KV_HEADS, t, :], start=True, stop=True)
            last.then_inc(a_scores, 1)

        def pe_a_turn(pe, u):
            pe.wait_ge(a_probs, u + 1)
            for r in range(GROUP):
                pe.transpose(ps[:, A_BANKS[0], r * P:(r + 1) * P], probs[:, r, 0:P], ident[:, :])
                last = pe.transpose(ps[0:EDGE, A_BANKS[1], r * P:(r + 1) * P], probs[:, r, P:A_KEYS], ident[:, :])
            last.then_inc(a_turned, 1)

        def pe_a_out(pe, u):
            t, o = u // A_KV_HEADS, HEAD_DIM * (u % A_KV_HEADS)
            pe.wait_ge(a_pt, 2 * u + 2)
            if u:
                pe.wait_ge(a_mixed, u)
            dst = ps[0:HEAD_DIM, A_OUT_BANK, 0:GROUP * P]
            pe.matmul(dst, v_nat[:, 0, t, o:o + HEAD_DIM], p_own.rearrange("p r q -> p (r q)"),
                      start=True, stop=False)
            pe.matmul(dst, v_edge[:, t, o:o + HEAD_DIM], p_edge.rearrange("p r q -> p (r q)"),
                      start=False, stop=True).then_inc(a_out, 1)

        def dve_a_max(dve, u):
            t = u // A_KV_HEADS
            dve.wait_ge(a_scores, u + 1)
            for r, hd, c, o in a_heads(u):
                at = A_KEYS * (r // 2)
                dve.scalar_tensor_tensor(probs[:, r, :], dist[:, t, :], -(2.0 ** (-8.0 * (hd + 1) / A_HEADS)),
                                         ps[:, A_BANKS[r % 2], at:at + A_KEYS], ALU.mult, ALU.add).then_inc(a_biased, 1)
            dve.wait_ge(a_biased, GROUP * (u + 1))
            sinks_u = sink_col[:, GROUP * (u % A_KV_HEADS):GROUP * (u % A_KV_HEADS + 1)]
            dve.tensor_reduce(row_max[:, :], probs[:, :, :], AX.X, ALU.max).then_inc(a_max, 1)
            dve.wait_ge(a_max, u + 1)
            dve.tensor_tensor(row_max[:, :], row_max[:, :], sinks_u, ALU.max).then_inc(a_sink_max, 1)
            dve.wait_ge(a_sink_max, u + 1)
            dve.tensor_scalar(neg_max[:, :], row_max[:, :], -1.0, None, ALU.mult).then_inc(a_neg, 1)
            dve.wait_ge(a_neg, u + 1)
            dve.tensor_tensor(sink_exp[:, :], neg_max[:, :], sinks_u, ALU.add).then_inc(a_sink_in, 1)

        def act_a_exp(act, u):
            act.wait_ge(a_sink_in, u + 1)
            for r in range(GROUP):
                act.activation(probs[:, r, :], probs[:, r, :], ACT.Exp, bias=neg_max[:, r:r + 1],
                               accum_out=row_sum[:, r:r + 1])
            act.activation(sink_exp[:, :], sink_exp[:, :], ACT.Exp).then_inc(a_exp, 1)

        def dve_a_probs(dve, u):
            dve.wait_ge(a_exp, u + 1)
            dve.tensor_tensor(row_sum[:, :], row_sum[:, :], sink_exp[:, :], ALU.add).then_inc(a_total, 1)
            dve.wait_ge(a_total, u + 1)
            dve.reciprocal(row_sum[:, :], row_sum[:, :]).then_inc(a_inv, 1)
            dve.wait_ge(a_inv, u + 1)
            dve.tensor_tensor(probs[:, :, :], probs[:, :, :],
                              row_sum[:, :].unsqueeze(2).to_broadcast([P, GROUP, A_KEYS]), ALU.mult).then_inc(a_probs, 1)

        def act_a_pt(act, u):
            act.wait_ge(a_turned, u + 1)
            if u:
                act.wait_ge(a_out, u)
            act.activation(p_own.rearrange("p r q -> p (r q)"), ps[:, A_BANKS[0], :], ACT.Copy).then_inc(a_pt, 1)
            act.activation(p_edge.rearrange("p r q -> p (r q)"), ps[0:EDGE, A_BANKS[1], :], ACT.Copy).then_inc(a_pt, 1)

        def dve_a_mixed(dve, u):
            t, g = u // A_KV_HEADS, u % A_KV_HEADS
            dve.wait_ge(a_out, u + 1)
            src = ps[0:HEAD_DIM, A_OUT_BANK, :].rearrange("d (c e q) -> d c e q", c=GROUP // 2, e=2)
            for e in range(2):
                c0 = g * GROUP // 2
                last = dve.tensor_copy(mixed[e * HEAD_DIM:(e + 1) * HEAD_DIM, c0:c0 + GROUP // 2, t * P:(t + 1) * P],
                                       src[:, :, e, :])
            last.then_inc(a_mixed, 1)

        def pe_b_scores(pe, hd):
            c, o = hd // 2, HEAD_DIM * (hd % 2)
            for j in range(B_TILES):
                if hd:
                    pe.wait_ge(b_stick, B_TILES * (hd - 1) + j + 1)
                for n, (kt, at) in enumerate(B_PARTS[j]):
                    w = SEQ - kt * P
                    last = pe.matmul(z_tile[j][:, at:at + w], kb[o:o + HEAD_DIM, c, kt * P:(kt + 1) * P],
                                     qb[o:o + HEAD_DIM, c, kt * P:SEQ], start=n == 0, stop=False,
                                     skip_group_check=True)
                last.then_inc(b_scores, 1)

        def pe_meta_scores(pe):
            for c in range(HC):
                last = pe.matmul(ps[:, META_BANK, :], k_meta[:, c, :], qb[:, c, :], start=c == 0, stop=False,
                                 skip_group_check=True)
            last.then_inc(m_scores, 1)

        def pe_b_logs(pe, hd):
            acc = dict(start=False, skip_group_check=True)
            for j in range(B_TILES):
                pe.wait_ge(b_masked, B_TILES * hd + j + 1)
                for kt, at in B_PARTS[j]:
                    pe.matmul(z_tile[j][:, at:at + P], ident_bf[:, :], future_bf[:, :], stop=False, **acc)
                last = pe.matmul(z_tile[j], neg_tri[:, :], sp[j][:, :], stop=False, **acc)
                if j == 0:
                    last = pe.matmul(z_tile[0][:, P:2 * P], neg_ones[:, :], sp[0][:, 2 * P:3 * P], stop=True, **acc)
                else:
                    pe.wait_ge(b_carry, 3 * hd + j)
                    last = pe.matmul(z_tile[j][:, P:B_COLS[j]], neg_ones[:, :], carry[j][:, :], stop=True, **acc)
                last.then_inc(b_logs, 1)
            if hd == 0:
                pe.wait_ge(m_soft, 1)
                pe.matmul(ps[:, META_BANK, :], neg_tri_meta[:, :], sp_meta[:, :], stop=False, **acc)
            pe.wait_ge(b_carry, 3 * hd + 3)
            at = P - N_META - N_META * hd
            pe.matmul(ps[:, META_BANK, :], neg_sel[:, at:at + P], carry[3][:, :], stop=hd == B_HEADS - 1,
                      **acc).then_inc(m_summed, 1)

        def pe_b_out(pe, hd):
            c, o = KC + hd // 2, HEAD_DIM * (hd % 2)
            pe.wait_ge(b_stick, B_TILES * (hd + 1))
            if hd >= 2:
                pe.wait_ge(b_mixed, hd // 2)
            parts = [(j, kt, at) for j in reversed(range(B_TILES)) for kt, at in B_PARTS[j]]
            for n, (j, kt, at) in enumerate(parts):
                last = pe.matmul(ps[o:o + HEAD_DIM, OUT_BANK, kt * P:SEQ], v_nat[:, c, kt, o:o + HEAD_DIM],
                                 stick[j][:, at:at + SEQ - kt * P], start=n == 0, stop=n == len(parts) - 1,
                                 skip_group_check=True)
            last.then_inc(b_out, 1)

        def pe_meta_out(pe):
            pe.wait_ge(m_stick, 1)
            pe.wait_ge(on_mean, 1)
            for c in range(HC):
                if c == HC - 1:
                    pe.wait_ge(b_mixed, HC)
                pe.matmul(ps[:, META_OUT_BANKS[c], :], v_meta[:, c, :], stick_meta[:, :], start=True,
                          stop=True).then_inc(m_out, 1)

        def ln_1_exp(act, dst, scores, done, wait):
            for step, (src, func, args) in enumerate(((scores, ACT.Abs, {}), (dst, ACT.Exp, dict(scale=-1.0)),
                                                      (dst, ACT.Ln, dict(bias=1.0)))):
                act.activation(dst, src, func, **args).then_inc(done[step], 1)
                if step < 2:
                    act.wait_ge(done[step], wait)

        def act_b_ln(act, hd):
            for j in range(B_TILES):
                act.wait_ge(b_scores, B_TILES * hd + j + 1)
                if hd and j == 0:
                    act.wait_ge(m_summed, hd)
                    act.wait_ge(b_carry, 3 * hd)
                ln_1_exp(act, sp[j][:, :], z_tile[j], (b_abs, b_exp, b_ln), B_TILES * hd + j + 1)

        def act_meta_ln(act):
            act.wait_ge(m_scores, 1)
            ln_1_exp(act, sp_meta[:, :], ps[:, META_BANK, :], (m_abs, m_exp, m_ln), 1)

        def dve_b_soft(dve, hd):
            for j in range(B_TILES):
                dve.wait_ge(b_ln, B_TILES * hd + j + 1)
                dve.scalar_tensor_tensor(sp[j][:, :], z_tile[j], 0.0, sp[j][:, :], ALU.max,
                                         ALU.add).then_inc(b_soft, 1)

        def dve_meta_soft(dve):
            dve.wait_ge(m_ln, 1)
            dve.scalar_tensor_tensor(sp_meta[:, :], ps[:, META_BANK, :], 0.0, sp_meta[:, :], ALU.max,
                                     ALU.add).then_inc(m_soft, 1)

        def pool_b(pool, hd):
            for j in range(B_TILES):
                pool.wait_ge(b_soft, B_TILES * hd + j + 1)
                for kt, at in B_PARTS[j]:
                    last = pool.tensor_tensor(sp[j][:, at:at + P], sp[j][:, at:at + P], causal[:, :], ALU.mult)
                last.then_inc(b_masked, 1)
                pool.wait_ge(b_masked, B_TILES * hd + j + 1)
                if hd:
                    pool.wait_ge(m_summed, hd)
                nxt = carry[j + 1]
                pool.tensor_copy(nxt[:, 0:P], sp[j][:, 0:P])
                if j == 0:
                    pool.tensor_tensor(nxt[:, P:2 * P], sp[0][:, P:2 * P], sp[0][:, 2 * P:3 * P],
                                       ALU.add).then_inc(b_carry, 1)
                else:
                    pool.wait_ge(b_carry, 3 * hd + j)
                    pool.tensor_tensor(nxt[:, P:B_COLS[j]], sp[j][:, P:B_COLS[j]], carry[j][:, :],
                                       ALU.add).then_inc(b_carry, 1)

        def act_b_stick(act, hd):
            if hd:
                act.wait_ge(b_out, hd)
            for j in range(B_TILES):
                act.wait_ge(b_logs, B_TILES * hd + j + 1)
                act.activation(stick[j][:, :], z_tile[j], ACT.Exp).then_inc(b_stick, 1)

        def act_meta_stick(act):
            act.wait_ge(m_summed, B_HEADS)
            act.activation(stick_meta[:, :], ps[:, META_BANK, :], ACT.Exp).then_inc(m_stick, 1)

        def dve_b_mixed(dve, c):
            dve.wait_ge(b_out, 2 * c + 2)
            dve.tensor_copy(mixed[:, QC + c, :], ps[:, OUT_BANK, :]).then_inc(b_mixed, 1)

        def dve_meta_mixed(dve):
            for c in range(HC):
                dve.wait_ge(m_out, c + 1)
                dve.wait_ge(b_mixed, c + 1)
                dve.tensor_tensor(mixed[:, QC + c, :], mixed[:, QC + c, :], ps[:, META_OUT_BANKS[c], :],
                                  ALU.add).then_inc(m_added, 1)

        def act_out_squares(act, g):
            for k in range(QC):
                n = g * QC + k
                if n >= 2:
                    act.wait_ge(on_added, n - 1)
                act.wait_ge(*((m_added, k + 1) if g else (a_mixed, UNITS)))
                act.activation(tmp_a[k % 2][:, 0:SEQ], mixed[:, n, :], ACT.Square).then_inc(on_sq, 1)

        def pool_out_sum(pool, g):
            for k in range(QC):
                n = g * QC + k
                pool.wait_ge(on_sq, n + 1)
                if k == 0:
                    pool.wait_ge(*((on_mean, 1) if g else (mean_done, 2)))
                    pool.tensor_copy(sq_sum[:, 0:SEQ], tmp_a[0][:, 0:SEQ]).then_inc(on_added, 1)
                else:
                    pool.wait_ge(on_added, n)
                    pool.tensor_tensor(sq_sum[:, 0:SEQ], sq_sum[:, 0:SEQ], tmp_a[k % 2][:, 0:SEQ],
                                       ALU.add).then_inc(on_added, 1)

        def pe_out_sum(pe, g):
            pe.wait_ge(on_added, QC * (g + 1))
            pe.wait_ge(*((m_added, 1) if g else (a_mixed, UNITS)))
            pe.matmul(ps[:, NORM_BANKS[g], :], ones[:, :], sq_sum[:, 0:SEQ], start=True, stop=True).then_inc(on_sum, 1)

        def dve_out_inv(dve, g):
            dve.wait_ge(on_sum, g + 1)
            dve.tensor_scalar(tmp_b[g][:, 0:SEQ], ps[:, NORM_BANKS[g], :], 1.0 / A_Q, EPS, ALU.mult,
                              ALU.add).then_inc(on_mean, 1)
            dve.wait_ge(on_mean, g + 1)
            dve.reciprocal(tmp_b[g][:, 0:SEQ], tmp_b[g][:, 0:SEQ]).then_inc(on_inv, 1)

        def act_out_hi(act, g):
            act.wait_ge(on_inv, g + 1)
            act.activation(tmp_b[g][:, 0:SEQ], tmp_b[g][:, 0:SEQ], ACT.Sqrt).then_inc(on_rms, 1)
            for c in range(g * QC, (g + 1) * QC):
                act.wait_ge(on_scaled, c + 1)
                act.activation(mix_hi[:, c, :], mixed[:, c, :], ACT.Copy,
                               scale=gains[:, G_OUT + c:G_OUT + c + 1]).then_inc(on_hi, 1)

        def dve_out_lo(dve, g):
            dve.wait_ge(on_rms, g + 1)
            for c in range(g * QC, (g + 1) * QC + 1):
                if c < (g + 1) * QC:
                    dve.tensor_tensor(mixed[:, c, :], mixed[:, c, :], tmp_b[g][:, 0:SEQ],
                                      ALU.mult).then_inc(on_scaled, 1)
                if c > g * QC:
                    dve.wait_ge(on_hi, c)
                    dve.wait_ge(on_scaled, c)
                    dve.scalar_tensor_tensor(mix_lo[:, c - 1, :], mixed[:, c - 1, :],
                                             gains[:, G_OUT + c - 1:G_OUT + c], mix_hi[:, c - 1, :].bitcast(F32),
                                             ALU.mult, ALU.subtract).then_inc(on_lo, 1)

        block = ctx.enter_context(nc.Block())

        @block.sync
        def _(sync):
            sync.dma_start(meta_in[:, :], meta_tokens).then_inc(meta_loaded, 16)
            gate0, up0 = pair_src(0, 0)
            for q in range(4):
                cols = slice(q * D // 4, (q + 1) * D // 4)
                sync.dma_start(x_in[:, :, cols], x[0].rearrange("(t p) n -> p t n", p=P)[:, :, cols]).then_inc(x_loaded[q], 16)
                if q == 1:
                    sync.dma_start(*gate0).then_inc(gate0_loaded, 16)
            for a in (0, DC // 2):
                sync.dma_start(*(t[:, a:a + DC // 2, :] for t in up0)).then_inc(raw_loaded[0], 16)
            load(sync, 1)
            with sync.Fori(1, FH) as it:
                load(sync, U_UP1, it)
                load(sync, U_UP1 + 1, it)
            with sync.Fori(0, DC // 2) as it:
                for k in range(4):
                    load(sync, U_DN1 + k, 2 * it)
            for n in range(U_IN, U_UP2):
                load(sync, n)
            with sync.Fori(0, FH) as it:
                load(sync, U_UP2, it)
                load(sync, U_UP2 + 1, it)
            with sync.Fori(0, DC // 2) as it:
                for k in range(4):
                    load(sync, U_DN2 + k, 2 * it)

        @block.gpsimd
        def _(pool):
            step = [0]

            def made(ins):
                step[0] += 1
                ins.then_inc(const_step, 1)
                pool.wait_ge(const_step, step[0])

            made(pool.memset(ones[:, :], 1.0))
            made(pool.memset(ident[:, :], 0.0))
            pool.affine_select(ident[:, :], ident[:, :], [[-1, P]], ALU.not_equal, 1.0, base=0,
                               channel_multiplier=1).then_inc(const_done, 1)
            for c in range(DC):
                pool.wait_ge(evacuated, M_X + c + 1)
                if c == 0:
                    pool.tensor_tensor(sq_sum[:, :], h[:, 0, :], h[:, 0, :], ALU.mult).then_inc(sq_added, 1)
                    continue
                pool.tensor_tensor(tmp_a[c % 2][:, :], h[:, c, :], h[:, c, :], ALU.mult).then_inc(sq_made, 1)
                pool.wait_ge(sq_made, c)
                pool.wait_ge(sq_added, c)
                pool.tensor_tensor(sq_sum[:, :], sq_sum[:, :], tmp_a[c % 2][:, :], ALU.add).then_inc(sq_added, 1)
            finish_sum(pool, DC, 0, T, first=True, taken=(mean_done, 1))
            for c in range(1, DC):
                finish_sum(pool, DC + c, c % 2, T)

            pool.wait_ge(acc_full, M_IN)
            made(pool.memset(head_ones[:, :], 0.0))
            for o in range(0, P, HEAD_DIM):
                made(pool.memset(head_ones[o:o + HEAD_DIM, o:o + HEAD_DIM], 1.0))
            pool.memset(neg_ones[:, :], -1.0)
            made(pool.memset(neg_tri[:, :], -1.0))
            made(pool.affine_select(neg_tri[:, :], neg_tri[:, :], [[-1, P]], ALU.is_ge, 0.0, base=0,
                                    channel_multiplier=1))
            blocks = neg_tri_meta.rearrange("p (b s) -> p b s", s=N_META)
            made(pool.affine_select(blocks, neg_tri.rearrange("p (b s) -> p b s", s=N_META),
                                    [[N_META, B_HEADS], [0, N_META]], ALU.is_ge, 0.0, base=N_META - 1,
                                    channel_multiplier=-1))
            made(pool.memset(neg_sel[:, :], 0.0))
            made(pool.memset(neg_sel[:, P - N_META:P], -1.0))
            made(pool.memset(k_meta[:, :, :], 0.0))
            made(pool.memset(v_pad[:, :, :], 0.0))
            made(pool.memset(causal[:, :], 1.0))
            made(pool.affine_select(causal[:, :], causal[:, :], [[1, P]], ALU.is_gt, 0.0, base=0,
                                    channel_multiplier=-1))
            made(pool.memset(future_bf[:, :], 0.0))
            made(pool.affine_select(future_bf[:, :], future_bf[:, :], [[1, P]], ALU.is_gt, -MASKED, base=0,
                                    channel_multiplier=-1))
            made(pool.tensor_copy(ident_bf[:, :], ident[:, :]))
            for t in range(TT):
                for lo, w, base in ((0, P, 0), (P, CHUNK, CHUNK), (P + CHUNK, N_META, N_META + t * P)):
                    last = pool.iota(dist[:, t, lo:lo + w], [[-1, w]], base=base, channel_multiplier=1,
                                     allow_small_or_imprecise_dtypes=True)
            last.then_inc(const_done, 1)
            for c in range(2 * HC):
                dst, src, chunk = (k_meta, kb, C_KB + c) if c < HC else (v_pad, v_t, C_VB + c - HC)
                c %= HC
                pool.wait_ge(evacuated, m_in["chunk", chunk] + 1)
                for e in range(2):
                    at = N_META * (2 * c + e)
                    rows = slice(e * HEAD_DIM, (e + 1) * HEAD_DIM)
                    last = pool.tensor_copy(dst[rows, c, at:at + N_META],
                                            src[rows, c if dst is k_meta else 1 + c, SEQ:T])
                last.then_inc(meta_padded, 1)
            for hd in range(B_HEADS):
                pool_b(pool, hd)
                if hd == B_HEADS - 2:
                    pool_out_sum(pool, 0)
            pool_out_sum(pool, 1)
            finish_sum(pool, 2 * DC, 0, SEQ, first=True, taken=(on_mean, 2))
            for c in range(1, DC):
                finish_sum(pool, 2 * DC + c, c % 2, SEQ)

        @block.tensor
        def _(pe):
            pe.wait_ge(const_done, 1)
            pe.wait_ge(small_loaded, SMALL)
            pe.transpose(ps[:, 7, 0:GAINS], gain_rows[:, :], ident[0:GAINS, 0:GAINS]).then_inc(gains_turned, 1)
            pe.wait_ge(meta_loaded, 16)
            for c in range(DC):
                pe.wait_ge(x_loaded[c * 4 // DC], 16)
                if c == 3:
                    pe.wait_ge(gains_done, 1)
                if c >= 4:
                    pe.wait_ge(evacuated, c - 3)
                b = 2 * (c % 4)
                for t in range(TT):
                    pe.transpose(ps[:, b, t * P:(t + 1) * P], x_in[:, t, c * P:(c + 1) * P], ident[:, :])
                pe.transpose(ps[:, b + 1, 0:N_META], meta_in[:, c * P:(c + 1) * P],
                             ident[0:N_META, 0:N_META]).then_inc(acc_full, 1)
            pe_up(pe, U_UP1, M_UP1, T, x_hi, x_lo, 0)
            with pe.Fori(0, DC // 2) as it:
                for k in range(2):
                    pe_down_chunk(pe, M_DN1 + 2 * k, U_DN1 + 2 * k, T, g1_hi, g1_lo, 0, dm=it)

            for use, k in in_uses:
                m = m_in[use, k]
                if (use, k) == ("norm", 0):
                    norm_sum(pe, m, T, 2 * DC)
                elif use == "chunk":
                    pair_chunk(pe, m, U_IN + k // 2, k % 2, in_cols(k), x_hi, x_lo,
                               fresh=(x_lo_done, DC) if k == 0 else None)
                elif use == "qk":
                    pe.wait_ge(qk_squared, k + 1)
                    pe.wait_ge(const_done, 2)
                    pe.wait_ge(evacuated, m - 3)
                    cols = in_cols(k)
                    dst = slot(m, cols)
                    for o, r in [(dst, slice(0, SEQ))] if cols == SEQ else [
                            (dst[:, a, :], slice(a * HALF, (a + 1) * HALF)) for a in range(2)]:
                        last = pe.matmul(o, head_ones[:, :], tmp_a[k % 2][:, r], start=True, stop=True)
                    last.then_inc(acc_full, 1)
                elif use == "v":
                    src = C_VA if k == 0 else C_VB + k - 1
                    pe.wait_ge(evacuated, max(m_in["chunk", src] + 1, m - 3))
                    b = 2 * (m % 4)
                    for t in range(TT):
                        pe.transpose(ps[:, b, t * P:(t + 1) * P], v_t[:, k, t * P:(t + 1) * P], ident[:, :])
                    if k == 0:
                        last = pe.transpose(ps[0:N_META, b + 1, 0:P], v_t[:, 0, SEQ:T], ident[:, :])
                    else:
                        pe.wait_ge(meta_padded, HC + k)
                        last = pe.transpose(ps[:, b + 1, 0:P], v_pad[:, k - 1, :], ident[:, :])
                    last.then_inc(acc_full, 1)

            pe.wait_ge(evacuated, M_HEADS)
            pe.wait_ge(k_win_done, 1)
            pe.wait_ge(v_edge_done, 1)
            pe.wait_ge(meta_padded, 2 * HC)
            pe_a_scores(pe, 0)
            pe_b_scores(pe, 0)
            pe_meta_scores(pe)
            pe_a_turn(pe, 0)
            pe_a_out(pe, 0)
            pe_a_scores(pe, 1)
            pe_b_logs(pe, 0)
            pe_a_turn(pe, 1)
            pe_a_out(pe, 1)
            for u in range(1, UNITS):
                ahead = u + 1 < UNITS
                if ahead:
                    pe_a_scores(pe, u + 1)
                pe_b_scores(pe, u)
                pe_b_out(pe, u - 1)
                if ahead:
                    pe_a_turn(pe, u + 1)
                else:
                    pe_out_sum(pe, 0)
                pe_b_logs(pe, u)
                if ahead:
                    pe_a_out(pe, u + 1)
            pe_b_out(pe, UNITS - 1)
            pe_meta_out(pe)


            def wo_chunk(d, part=None):
                pair_chunk(pe, M_WO + d, U_WO + d // 2, d % 2, SEQ, mix_hi, mix_lo, part=part, fresh=(on_lo, 0),
                           skipped=0 if d else M_WO - M_HEADS)

            for d in range(2):
                wo_chunk(d, range(QC))
            pe_out_sum(pe, 1)
            for d in range(2):
                wo_chunk(d, range(QC, MC))
            for d in range(2, DC):
                wo_chunk(d)

            pe_up(pe, U_UP2, M_UP2, SEQ, x2_hi, x2_lo, 2 * DC)

            def turn_out(par, d):
                pe.wait_ge(evacuated, 2 * d + M_DN2 + 2)
                if not isinstance(d, int) or d >= 2:
                    pe.wait_ge(out_staged, d - 1)
                b = 2 * ((M_DN2 + 2 * par + 1) % 4)
                for t in range(TT):
                    last = pe.transpose(ps[:, b, t * P:(t + 1) * P], tmp_b[par][:, t * P:(t + 1) * P], ident[:, :])
                last.then_inc(out_turned, 1)

            def down_out(k, it=0, turn=True):
                between = (lambda: turn_out(1 - k, 2 * it + k - 1)) if turn else None
                pe_down_chunk(pe, M_DN2 + 2 * k, U_DN2 + 2 * k, SEQ, g2_hi, g2_lo, FC, dm=it, between=between)

            down_out(0, turn=False)
            down_out(1)
            with pe.Fori(1, DC // 2) as it:
                down_out(0, it)
                down_out(1, it)
            turn_out(1, DC - 1)

        @block.scalar
        def _(act):
            row = 0
            for src in (ffn1_norm_g, mix_norm_g, ffn2_norm_g, attn_out_g, sb_out_g):
                rows = src.shape[1] // P
                act.dma_start(gain_rows[row:row + rows, :],
                              src[0].rearrange("(c p) -> c p", p=P)).then_inc(small_loaded, 16)
                row += rows
            for k, src in enumerate((q_norm_g, k_norm_g)):
                for o in range(0, P, HEAD_DIM):
                    act.dma_start(gain_rows[row + k:row + k + 1, o:o + HEAD_DIM], src).then_inc(small_loaded, 16)
            act.dma_start(sink_col[:, :], sinks.to_broadcast([P, A_HEADS])).then_inc(small_loaded, 16)
            act.wait_ge(gains_done, 2)
            pair0, pair0_hi = (t[0].rearrange("p (c w o) -> p c w o", c=DC, w=2) for t in (raw, w_hi))
            for c in range(DC):
                finish_hi(act, G_FFN1, c, c % 2, c, T, x_hi, M_X + c + 1, squares=False)
                if c == DC // 2 - 1:
                    act.wait_ge(gate0_loaded, 16)
                    act.activation(pair0_hi[:, :, 0, :], pair0[:, :, 0, :], ACT.Copy).then_inc(gate0_hi, 1)
            act.wait_ge(raw_loaded[0], 32)
            act.activation(pair0_hi[:, :, 1, :], pair0[:, :, 1, :], ACT.Copy).then_inc(hi_split, 1)
            act_up(act, U_UP1, M_UP1, 0, T, g1_hi, 0)

            def down(k, it):
                split_hi(act, U_DN1 + 2 * k + 1, 2 * it, step=2)
                split_hi(act, U_DN1 + 2 * k + 2, 2 * it, step=2)
                finish_hi(act, G_MIX, 2 * it + DC + k, k, 2 * it + k, T, x_hi, 4 * it + M_DN1 + 2 * k + 2)

            with act.Fori(0, DC // 2 - 1) as it:
                down(0, it)
                down(1, it)
            down(0, DC // 2 - 1)
            down(1, DC // 2 - 1)

            for use, k in in_uses:
                m = m_in[use, k]
                if use == "chunk":
                    if k % 2 == 0:
                        split_hi(act, U_IN + k // 2 + 1)
                    if k == 0:
                        rms_act(act, T, 1)
                    if k % 2 == 0 and QC <= k < QC + 2 * (QC + KC):
                        n = (k - QC) // 2
                        cols = in_cols(n)
                        act.wait_ge(evacuated, m_in["chunk", n] + 1)
                        if n >= 2:
                            act.wait_ge(acc_full, m_in["qk", n - 2] + 1)
                        act.activation(tmp_a[n % 2][:, 0:cols], qa[:, n, :] if n < QC else k_a[:, :],
                                       ACT.Square).then_inc(qk_squared, 1)
                elif use == "qk":
                    cols = in_cols(k)
                    act.wait_ge(qk_inv, k + 1)
                    act.activation(tmp_b[k % 2][:, 0:cols], tmp_b[k % 2][:, 0:cols], ACT.Sqrt).then_inc(qk_rms, 1)
            act.wait_ge(qk_done, QC + KC)
            for g in range(A_KV_HEADS):
                src = k_a[g * HEAD_DIM:(g + 1) * HEAD_DIM, :]
                for e in range(2):
                    dst = k_win[e * HEAD_DIM:(e + 1) * HEAD_DIM, g, :, :]
                    act.activation(dst[:, :, 0:P], src[:, 0:SEQ].rearrange("p (t c) -> p t c", c=P), ACT.Copy)
                    act.activation(dst[:, 0, P:P + CHUNK], src[:, 0:CHUNK], ACT.Copy)
                    before = src[:, CHUNK:SEQ - CHUNK].rearrange("p (t c) -> p t c", c=P)[:, :, 0:CHUNK]
                    act.activation(dst[:, 1:TT, P:P + CHUNK], before, ACT.Copy)
                    last = act.activation(dst[:, :, P + CHUNK:A_KEYS],
                                          src[:, SEQ:T].unsqueeze(1).to_broadcast([HEAD_DIM, TT, N_META]), ACT.Copy)
            last.then_inc(k_win_done, 1)

            act.preload_act_table_set(LN_EXP)
            act_a_exp(act, 0)
            act_b_ln(act, 0)
            act_meta_ln(act)
            act_a_pt(act, 0)
            act_a_exp(act, 1)
            act_b_stick(act, 0)
            act_a_pt(act, 1)
            for u in range(1, UNITS):
                ahead = u + 1 < UNITS
                if ahead:
                    act_a_exp(act, u + 1)
                act_b_ln(act, u)
                if ahead:
                    act_a_pt(act, u + 1)
                else:
                    act_out_squares(act, 0)
                act_b_stick(act, u)
            act_meta_stick(act)
            act_out_hi(act, 0)
            act_out_squares(act, 1)
            act_out_hi(act, 1)
            for d in range(DC):
                if d % 2 == 0:
                    split_hi(act, U_WO + d // 2 + 1)
                finish_hi(act, G_FFN2, 2 * DC + d, d % 2, d, SEQ, x2_hi, M_WO + d + 1)
            act_up(act, U_UP2, M_UP2, FC, SEQ, g2_hi, 2)

            def stage(par, d, uses):
                act.wait_ge(out_turned, d + 1)
                if not isinstance(d, int) or d >= 2:
                    act.wait_ge(out_written[par], uses)
                b = 2 * ((M_DN2 + 2 * par + 1) % 4)
                act.activation(tmp_a[par][:, 0:SEQ], ps[:, b, :], ACT.Copy).then_inc(out_staged, 1)
                act.wait_ge(out_staged, d + 1)
                act.dma_start(out[0].rearrange("(t p) n -> p t n", p=P)[:, :, bass.ds(d * P, P)],
                              tmp_a[par][:, 0:SEQ].rearrange("p (t n) -> p t n", n=P)).then_inc(out_written[par], 16)

            def down_out(k, it=0, out_chunk=True):
                split_hi(act, U_DN2 + 2 * k + 1, 2 * it, step=2)
                split_hi(act, U_DN2 + 2 * k + 2, 2 * it, step=2)
                if out_chunk:
                    stage(1 - k, 2 * it + k - 1, 16 * (it if k else it - 1))

            down_out(0, out_chunk=False)
            down_out(1)
            with act.Fori(1, DC // 2 - 1) as it:
                down_out(0, it)
                down_out(1, it)
            for k in range(2):
                d = DC - 2 + k
                split_hi(act, U_DN2 + 2 * d + 1)
                split_hi(act, U_DN2 + 2 * d + 2)
                stage(1 - k, d - 1, 16 * ((d - 1) // 2))
            stage(1, DC - 1, 16 * ((DC - 1) // 2))
            for s in range(2):
                act.wait_ge(out_written[s], 16 * DC // 2)

        @block.vector
        def _(dve):
            pair0, pair0_hi, pair0_lo = (t[0].rearrange("p (c w o) -> p c w o", c=DC, w=2)
                                         for t in (raw, w_hi, w_lo))
            dve.wait_ge(gains_turned, 1)
            dve.tensor_copy(gains[:, :], ps[:, 7, 0:GAINS]).then_inc(gains_done, 1)
            dve.wait_ge(gains_done, 1)
            dve.tensor_scalar(head_gain[:, 0:1], head_gain[:, 0:1], SCALE, None, ALU.mult).then_inc(gains_done, 1)
            for c in range(DC + 1):
                if c < DC:
                    b = 2 * (c % 4)
                    dve.wait_ge(acc_full, M_X + c + 1)
                    dve.tensor_copy(h[:, c, 0:SEQ], ps[:, b, 0:SEQ])
                    dve.tensor_copy(h[:, c, SEQ:T], ps[:, b + 1, 0:N_META]).then_inc(evacuated, 1)
                if c:
                    finish_lo(dve, G_FFN1, c - 1, c - 1, T, x_hi, x_lo)
                if c == DC // 2:
                    dve.wait_ge(gate0_hi, 1)
                    dve.tensor_tensor(pair0_lo[:, :, 0, :], pair0[:, :, 0, :], pair0_hi[:, :, 0, :].bitcast(F32),
                                      ALU.subtract).then_inc(gate0_lo, 1)
            dve.wait_ge(hi_split, 1)
            dve.tensor_tensor(pair0_lo[:, :, 1, :], pair0[:, :, 1, :], pair0_hi[:, :, 1, :].bitcast(F32),
                              ALU.subtract).then_inc(lo_split, 1)
            dve_up(dve, U_UP1, M_UP1, 0, T, g1_hi, g1_lo, 0)

            def add_chunk(m, d, cols, half, dm=0, uses=2, frees=2):
                dve.wait_ge(acc_full, 4 * dm + m + uses)
                row = tok(h, d, cols)
                dve.scalar_tensor_tensor(row, slot(m, cols), half, row, ALU.mult, ALU.add).then_inc(evacuated, frees)

            def down(k, it):
                split_lo(dve, U_DN1 + 2 * k + 1, 2 * it)
                split_lo(dve, U_DN1 + 2 * k + 2, 2 * it)
                add_chunk(M_DN1 + 2 * k, 2 * it + k, T, 0.5, dm=it)
                finish_lo(dve, G_MIX, 2 * it + DC + k, 2 * it + k, T, x_hi, x_lo)

            with dve.Fori(0, DC // 2 - 1) as it:
                down(0, it)
                down(1, it)
            down(0, DC // 2 - 1)
            down(1, DC // 2 - 1)

            def head_norm(k):
                dve.wait_ge(qk_rms, k + 1)
                row = qa[:, k, :] if k < QC else k_a[:, :]
                gain = head_gain[:, 0:1] if k < QC else head_gain[:, 1:2]
                dve.scalar_tensor_tensor(row, row, gain, tmp_b[k % 2][:, 0:in_cols(k)], ALU.mult,
                                         ALU.mult).then_inc(qk_done, 1)

            dve.wait_ge(gains_done, 2)
            for use, k in in_uses:
                m = m_in[use, k]
                if use == "chunk":
                    if k % 2 == 0:
                        split_lo(dve, U_IN + k // 2 + 1)
                    if k == 0:
                        rms_dve(dve, m + 1, T, 1)
                        dve.wait_ge(rms_done, 2)
                    dve.wait_ge(acc_full, m + 1)
                    dst = (qa[:, k, :] if k < C_KA else k_a[:, :] if k < C_VA else v_t[:, 0, :] if k < C_QB else
                           qb[:, k - C_QB, :] if k < C_KB else kb[:, k - C_KB, :] if k < C_VB else
                           v_t[:, 1 + k - C_VB, :])
                    cols = in_cols(k)
                    dve.scalar_tensor_tensor(wide(dst, cols), slot(m, cols), SCALE if C_QB <= k < C_KB else 1.0,
                                             wide(rms_inv[:, 0:cols], cols), ALU.mult,
                                             ALU.mult).then_inc(evacuated, 3 if k == 0 else 1)
                elif use == "qk":
                    dve.wait_ge(acc_full, m + 1)
                    if k >= 1:
                        head_norm(k - 1)
                    cols = in_cols(k)
                    dve.tensor_scalar(wide(tmp_b[k % 2][:, 0:cols], cols), slot(m, cols), 1.0 / HEAD_DIM, EPS, ALU.mult,
                                      ALU.add).then_inc(evacuated, 1)
                    dve.wait_ge(evacuated, m + 1)
                    dve.reciprocal(tmp_b[k % 2][:, 0:cols], tmp_b[k % 2][:, 0:cols]).then_inc(qk_inv, 1)
                elif use == "v":
                    if k == 0:
                        head_norm(QC)
                    dve.wait_ge(acc_full, m + 1)
                    b = 2 * (m % 4)
                    dve.tensor_copy(v_nat[:, k, :, :].rearrange("p t n -> p (t n)"), ps[:, b, :])
                    meta = va_meta[:, :] if k == 0 else v_meta[:, k - 1, :]
                    dve.tensor_copy(meta, ps[0:meta.shape[0], b + 1, 0:P]).then_inc(evacuated, 1)
                    if k == 0:
                        dve.wait_ge(evacuated, m + 1)
                        dve.tensor_copy(v_edge[0:HEAD_DIM, 0, :], v_nat[0:HEAD_DIM, 0, 0, :])
                        dve.tensor_copy(v_edge[0:HEAD_DIM, 1:TT, :], v_nat[HEAD_DIM:P, 0, 0:TT - 1, :])
                        for t in range(TT):
                            last = dve.tensor_copy(v_edge[HEAD_DIM:EDGE, t, :], va_meta[:, :])
                        last.then_inc(v_edge_done, 1)

            dve.wait_ge(const_done, 2)
            dve.scalar_tensor_tensor(dist[:, :, :], dist[:, :, :], -1.0, dist[:, :, :], ALU.mult,
                                     ALU.max).then_inc(dist_done, 1)
            dve.wait_ge(dist_done, 1)
            dve.memset(dist[0:CHUNK, :, CHUNK:P], MASKED)
            dve.memset(dist[CHUNK:P, :, P:P + CHUNK], MASKED)
            dve.memset(dist[0:CHUNK, 0, P:P + CHUNK], MASKED).then_inc(dist_done, 1)
            dve.wait_ge(dist_done, 2)
            dve_a_max(dve, 0)
            dve_a_probs(dve, 0)
            dve_b_soft(dve, 0)
            dve_meta_soft(dve)
            dve_a_mixed(dve, 0)
            dve_a_max(dve, 1)
            dve_a_probs(dve, 1)
            dve_a_mixed(dve, 1)
            for u in range(1, UNITS):
                ahead = u + 1 < UNITS
                if ahead:
                    dve_a_max(dve, u + 1)
                    dve_a_probs(dve, u + 1)
                dve_b_soft(dve, u)
                if u % 2 == 0:
                    dve_b_mixed(dve, u // 2 - 1)
                if ahead:
                    dve_a_mixed(dve, u + 1)
                else:
                    dve_out_inv(dve, 0)
            dve_b_mixed(dve, HC - 1)
            dve_out_lo(dve, 0)
            dve_meta_mixed(dve)
            dve_out_inv(dve, 1)
            dve_out_lo(dve, 1)
            for d in range(DC):
                if d % 2 == 0:
                    split_lo(dve, U_WO + d // 2 + 1)
                add_chunk(M_WO + d, d, SEQ, 1.0, uses=1, frees=1 if d else 1 + M_WO - M_HEADS)
                finish_lo(dve, G_FFN2, 2 * DC + d, d, SEQ, x2_hi, x2_lo)
            dve_up(dve, U_UP2, M_UP2, FC, SEQ, g2_hi, g2_lo, 2)

            def down_out(k, it):
                split_lo(dve, U_DN2 + 2 * k + 1, 2 * it)
                split_lo(dve, U_DN2 + 2 * k + 2, 2 * it)
                m, d = M_DN2 + 2 * k, 2 * it + k
                dve.wait_ge(acc_full, 4 * it + m + 2)
                if not isinstance(it, int) or it:
                    dve.wait_ge(out_turned, d - 1)
                dve.scalar_tensor_tensor(tmp_b[k][:, 0:SEQ], slot(m, SEQ), 0.5, tok(h, d, SEQ), ALU.mult,
                                         ALU.add).then_inc(evacuated, 2)

            down_out(0, 0)
            down_out(1, 0)
            with dve.Fori(1, DC // 2 - 1) as it:
                down_out(0, it)
                down_out(1, it)
            down_out(0, DC // 2 - 1)
            down_out(1, DC // 2 - 1)


_INS = ["x", "meta_tokens", "ffn1_norm_g", "ffn1_w_gate", "ffn1_w_up", "ffn1_w_down", "mix_norm_g", "w_in",
        "q_norm_g", "k_norm_g", "sinks", "attn_out_g", "sb_out_g", "w_o",
        "ffn2_norm_g", "ffn2_w_gate", "ffn2_w_up", "ffn2_w_down"]


def kernel(**inputs):
    import numpy as _np
    import concourse.bacc as _bacc
    from concourse import mybir as _mybir
    from concourse.bass_utils import run_bass_kernel_spmd as _run

    nc = _bacc.Bacc("TRN2", target_bir_lowering=False, num_devices=1)
    arrays, args = {}, []
    for name in _INS:
        a = _np.ascontiguousarray(inputs[name])
        arrays[f"in_{name}_dram"] = a
        args.append(nc.dram_tensor(f"in_{name}_dram", a.shape, _mybir.dt.from_np(a.dtype), kind="ExternalInput").ap())
    shape = tuple(inputs["x"].shape)
    out = nc.dram_tensor("out_0_dram", shape, _mybir.dt.from_np(_np.dtype("float32")), kind="ExternalOutput").ap()
    hybrid_layer_kernel(nc, *args, out)
    r = _run(nc, [arrays], core_ids=[0])
    return r.results[0]["out_0_dram"]
```
